# Optimizing a Trainium2 kernel written in Bass

```python
import math
import jax, jax.numpy as jnp
from jax import lax
import numpy as np
import jax
import jax.numpy as jnp

D_MODEL = 1024
BATCH = 1
SEQ = 256
DEPTH = 2

N_MIXERS = 2
N_RET = (DEPTH + 1) // 2
N_LRU = DEPTH // 2

RET_HEADS = D_MODEL // 256
RET_DK = 256
RET_DV = 2 * RET_DK
RET_QK_W = RET_HEADS * RET_DK
RET_V_W = RET_HEADS * RET_DV
RET_CHUNK = 128
ROPE_BASE = 10000.0

LRU_WIDTH = 1536
LRU_BLOCK = 256
LRU_BLOCKS = LRU_WIDTH // LRU_BLOCK
LRU_CONV = 4
LRU_C = 8.0

D_FF = ((8 * D_MODEL // 3 + 255) // 256) * 256

NORM_EPS = 1e-6


def rms_norm(x, g):
    xf = x.astype(jnp.float32)
    y = xf * lax.rsqrt(jnp.mean(xf * xf, axis=-1, keepdims=True) + NORM_EPS)
    return (y * g.astype(jnp.float32)).astype(x.dtype)

def rope(x, pos):
    half = x.shape[-1] // 2
    inv = 1.0 / (ROPE_BASE ** (jnp.arange(half, dtype=jnp.float32) / half))
    ang = pos.astype(jnp.float32)[:, None] * inv[None, :]
    cos = jnp.cos(ang)[None, :, None, :]
    sin = jnp.sin(ang)[None, :, None, :]
    x1, x2 = x[..., :half], x[..., half:]
    return jnp.concatenate([x1 * cos - x2 * sin, x1 * sin + x2 * cos], axis=-1)

def retention_mixer(x, w_in, w_out):
    B, S, _ = x.shape
    H, DK, DV, C = RET_HEADS, RET_DK, RET_DV, RET_CHUNK
    N = S // C
    proj = x @ w_in
    q, k, v, g = jnp.split(proj, [RET_QK_W, 2 * RET_QK_W, 2 * RET_QK_W + RET_V_W], axis=-1)
    pos = jnp.arange(S)
    q = rope(q.reshape(B, S, H, DK).astype(jnp.float32), pos)
    k = rope(k.reshape(B, S, H, DK).astype(jnp.float32), pos) * (DK ** -0.5)
    v = v.reshape(B, S, H, DV).astype(jnp.float32)

    log_gamma = jnp.log1p(-jnp.exp2(-5.0 - jnp.arange(H, dtype=jnp.float32)))
    idx = jnp.arange(C, dtype=jnp.float32)
    rel = idx[:, None] - idx[None, :]
    causal = rel >= 0
    decay = jnp.where(causal[None],
                      jnp.exp(jnp.where(causal, rel, 0.0)[None] * log_gamma[:, None, None]),
                      0.0)
    q_decay = jnp.exp((idx[:, None] + 1.0) * log_gamma[None, :])
    k_decay = jnp.exp((C - 1.0 - idx[:, None]) * log_gamma[None, :])
    chunk_decay = jnp.exp(C * log_gamma)

    qc = q.reshape(B, N, C, H, DK)
    kc = k.reshape(B, N, C, H, DK)
    vc = v.reshape(B, N, C, H, DV)

    scores = jnp.einsum('bnqhd,bnkhd->bnhqk', qc, kc) * decay[None, None]
    intra = jnp.einsum('bnhqk,bnkhe->bnqhe', scores, vc)

    def step(state, inp):
        qi, ki, vi = inp
        out = jnp.einsum('bchd,bhde->bche', qi, state) * q_decay[None, :, :, None]
        state = state * chunk_decay[None, :, None, None] + jnp.einsum(
            'bchd,bche->bhde', ki * k_decay[None, :, :, None], vi)
        return state, out

    state0 = jnp.zeros((B, H, DK, DV), jnp.float32)
    _, inter = lax.scan(step, state0, (qc.transpose(1, 0, 2, 3, 4),
                                       kc.transpose(1, 0, 2, 3, 4),
                                       vc.transpose(1, 0, 2, 3, 4)))
    o = (intra + inter.transpose(1, 0, 2, 3, 4)).reshape(B, S, H, DV)

    mu = jnp.mean(o, axis=-1, keepdims=True)
    oc = o - mu
    o = oc * lax.rsqrt(jnp.mean(oc * oc, axis=-1, keepdims=True) + NORM_EPS)
    o = o.reshape(B, S, RET_V_W).astype(x.dtype) * jax.nn.silu(g)
    return o @ w_out

def rglru_mixer(x, w_in, conv_w, conv_b, gate_w, gate_b, a_param, w_out):
    B, S, _ = x.shape
    proj = x @ w_in
    y_branch, u = jnp.split(proj, 2, axis=-1)
    y_branch = jax.nn.gelu(y_branch, approximate=True)

    u = lax.conv_general_dilated(
        u, conv_w[:, None, :], window_strides=(1,), padding=[(LRU_CONV - 1, 0)],
        dimension_numbers=('NWC', 'WIO', 'NWC'), feature_group_count=LRU_WIDTH) + conv_b

    ub = u.reshape(B, S, LRU_BLOCKS, LRU_BLOCK)
    gates = jnp.einsum('bsnk,gnkj->gbsnj', ub, gate_w) + gate_b[:, None, None]
    gates = jax.nn.sigmoid(gates.astype(jnp.float32)).reshape(2, B, S, LRU_WIDTH)
    r, i = gates[0], gates[1]

    log_a = -LRU_C * r * jax.nn.softplus(-a_param.astype(jnp.float32))
    a = jnp.exp(log_a)
    mult = jnp.sqrt(-jnp.expm1(2.0 * log_a))
    b = mult * (i * u.astype(jnp.float32))

    def combine(lhs, rhs):
        a1, b1 = lhs
        a2, b2 = rhs
        return a1 * a2, a2 * b1 + b2

    _, h = lax.associative_scan(combine, (a, b), axis=1)
    return (h.astype(x.dtype) * y_branch) @ w_out

def swiglu_ffn(x, w_in, w_out):
    gate, up = jnp.split(x @ w_in, 2, axis=-1)
    return (jax.nn.silu(gate) * up) @ w_out

def first_inputs(seed: int = 0) -> dict:
    key = jax.random.key(seed)
    ks = jax.random.split(key, 16)
    f32 = jnp.float32

    def normal(k, shape, fan_in):
        return jax.random.normal(k, shape, f32) * (fan_in ** -0.5)

    x = jax.random.normal(ks[0], (BATCH, SEQ, D_MODEL), f32)
    ret_w_in = normal(ks[1], (N_RET, D_MODEL, 2 * RET_QK_W + 2 * RET_V_W), D_MODEL)
    ret_w_out = normal(ks[2], (N_RET, RET_V_W, D_MODEL), RET_V_W)
    lru_w_in = normal(ks[3], (N_LRU, D_MODEL, 2 * LRU_WIDTH), D_MODEL)
    lru_conv_w = normal(ks[4], (N_LRU, LRU_CONV, LRU_WIDTH), LRU_CONV)
    lru_conv_b = 0.01 * jax.random.normal(ks[5], (N_LRU, LRU_WIDTH), f32)
    lru_gate_w = normal(ks[6], (N_LRU, 2, LRU_BLOCKS, LRU_BLOCK, LRU_BLOCK), LRU_BLOCK)
    lru_gate_b = 0.01 * jax.random.normal(ks[7], (N_LRU, 2, LRU_BLOCKS, LRU_BLOCK), f32)
    a0 = jax.random.uniform(ks[8], (N_LRU, LRU_WIDTH), f32, minval=0.9, maxval=0.999)
    lru_a_param = jnp.log(a0) - jnp.log1p(-a0)
    lru_w_out = normal(ks[9], (N_LRU, LRU_WIDTH, D_MODEL), LRU_WIDTH)
    norm_g = 1.0 + 0.02 * jax.random.normal(ks[10], (DEPTH, 4, D_MODEL), f32)
    ffn_w_in = normal(ks[11], (DEPTH, D_MODEL, 2 * D_FF), D_MODEL)
    ffn_w_out = normal(ks[12], (DEPTH, D_FF, D_MODEL), D_FF)
    return {"x": x, "ret_w_in": ret_w_in, "ret_w_out": ret_w_out,
            "lru_w_in": lru_w_in, "lru_conv_w": lru_conv_w, "lru_conv_b": lru_conv_b,
            "lru_gate_w": lru_gate_w, "lru_gate_b": lru_gate_b, "lru_a_param": lru_a_param,
            "lru_w_out": lru_w_out, "norm_g": norm_g,
            "ffn_w_in": ffn_w_in, "ffn_w_out": ffn_w_out}

def first_block(x, ret_w_in, ret_w_out, lru_w_in, lru_conv_w, lru_conv_b, lru_gate_w,
              lru_gate_b, lru_a_param, lru_w_out, norm_g, ffn_w_in, ffn_w_out):
    for layer in range(DEPTH):
        j = layer // N_MIXERS
        h = rms_norm(x, norm_g[layer, 0])
        if layer % N_MIXERS == 0:
            m = retention_mixer(h, ret_w_in[j], ret_w_out[j])
        else:
            m = rglru_mixer(h, lru_w_in[j], lru_conv_w[j], lru_conv_b[j], lru_gate_w[j],
                            lru_gate_b[j], lru_a_param[j], lru_w_out[j])
        x = x + rms_norm(m, norm_g[layer, 1])
        f = swiglu_ffn(rms_norm(x, norm_g[layer, 2]), ffn_w_in[layer], ffn_w_out[layer])
        x = x + rms_norm(f, norm_g[layer, 3])
    return x


DEPTH_2 = 1

GRID_W = 64
CTX_LEN = 256
D_SSD = D_MODEL
SSD_HEADDIM = 64
SSD_HEADS = D_SSD // SSD_HEADDIM
SSD_GROUPS = 4
SSD_HEADS_PER_GROUP = SSD_HEADS // SSD_GROUPS
SSD_STATE = 128
CONV_W = 5
CHUNK = 128
CONV_DIM = D_SSD + 2 * SSD_GROUPS * SSD_STATE
D_FOURIER = D_MODEL // 2
FOURIER_GROUPS = 4
FOURIER_CH = D_FOURIER // FOURIER_GROUPS
D_MIX = D_SSD + D_FOURIER
D_PROJ = D_SSD + CONV_DIM + 2 * SSD_HEADS + D_FOURIER
N_EXPERT_GROUPS = 4
EXPERTS_PER_GROUP = 8
N_EXPERTS = N_EXPERT_GROUPS * EXPERTS_PER_GROUP
TOP_K_INNER = 2
D_EXPERT = D_MODEL // 2
EXPERT_BLOCK = 128
EPS = 1e-6


def rmsnorm(u, w):
    uf = u.astype(jnp.float32)
    uf = uf * lax.rsqrt(jnp.mean(uf * uf, axis=-1, keepdims=True) + EPS)
    return uf.astype(u.dtype) * w

def modulate(u, shift, scale):
    return u * (1 + scale) + shift

def depthwise_conv(u, w):
    return lax.conv_general_dilated(u, w[:, None, :], window_strides=(1,), padding='SAME',
                                    dimension_numbers=('NWC', 'WIO', 'NWC'),
                                    feature_group_count=u.shape[-1])

def ssd_scan(xd, da, bm, cm, h0):
    out_dtype = xd.dtype
    b, l = xd.shape[0], xd.shape[1]
    nc = l // CHUNK
    g, r, p, n = SSD_GROUPS, SSD_HEADS_PER_GROUP, SSD_HEADDIM, SSD_STATE
    f32 = jnp.float32
    xd = xd.astype(f32).reshape(b, nc, CHUNK, g, r, p)
    da = da.astype(f32).reshape(b, nc, CHUNK, g, r)
    bm = bm.astype(f32).reshape(b, nc, CHUNK, g, n)
    cm = cm.astype(f32).reshape(b, nc, CHUNK, g, n)
    a_cs = jnp.cumsum(da, axis=2)
    a_lr = jnp.moveaxis(a_cs, 2, -1)
    lower = jnp.tril(jnp.ones((CHUNK, CHUNK), bool))
    seg = jnp.where(lower, a_lr[..., :, None] - a_lr[..., None, :], -jnp.inf)
    cb = jnp.einsum('bclgn,bcsgn->bcgls', cm, bm)
    y_diag = jnp.einsum('bcgrls,bcsgrp->bclgrp', cb[:, :, :, None] * jnp.exp(seg), xd)
    decay_to_end = jnp.exp(a_cs[:, :, -1:] - a_cs)
    chunk_states = jnp.einsum('bcqgn,bcqgrp->bcgrpn', bm, xd * decay_to_end[..., None])
    chunk_decay = jnp.exp(a_cs[:, :, -1])

    def carry_state(h, inp):
        dec, st = inp
        return h * dec[..., None, None] + st, h

    h_final, h_in = lax.scan(carry_state, h0.astype(f32),
                             (jnp.moveaxis(chunk_decay, 1, 0), jnp.moveaxis(chunk_states, 1, 0)))
    h_in = jnp.moveaxis(h_in, 0, 1)
    y_off = jnp.einsum('bcqgn,bcgrpn->bcqgrp', cm, h_in) * jnp.exp(a_cs)[..., None]
    y = (y_diag + y_off).reshape(b, l, SSD_HEADS, p)
    return y.astype(out_dtype), h_final

def ssd_mixer(z, xbc, dt_raw, h0_f, h0_b, conv_w, conv_b, dt_bias, a_log, d_skip, norm_w):
    b, l = xbc.shape[0], xbc.shape[1]
    xbc = jax.nn.silu(depthwise_conv(xbc, conv_w) + conv_b)
    xs, bm, cm = jnp.split(xbc, [D_SSD, D_SSD + SSD_GROUPS * SSD_STATE], axis=-1)
    xs = xs.reshape(b, l, SSD_HEADS, SSD_HEADDIM)
    bm = bm.reshape(b, l, SSD_GROUPS, SSD_STATE)
    cm = cm.reshape(b, l, SSD_GROUPS, SSD_STATE)
    dt = jax.nn.softplus(dt_raw.reshape(b, l, 2, SSD_HEADS) + dt_bias)
    da = dt * -jnp.exp(a_log)
    flip = lambda u: jnp.flip(u, axis=1)
    y_f, h_f = ssd_scan(xs * dt[:, :, 0, :, None], da[:, :, 0], bm, cm, h0_f)
    y_b, h_b = ssd_scan(flip(xs * dt[:, :, 1, :, None]), flip(da[:, :, 1]), flip(bm), flip(cm), h0_b)
    y = y_f + flip(y_b) + d_skip[:, None] * xs
    y = y.reshape(b, l, D_SSD) * jax.nn.silu(z)
    return rmsnorm(y, norm_w), h_f, h_b

def fourier_mixer(f, w_four):
    b, l = f.shape[0], f.shape[1]
    fg = f.reshape(b, l, FOURIER_GROUPS, FOURIER_CH).astype(jnp.float32)
    spec = jnp.fft.fft2(fg, axes=(1, 3), norm='ortho').real.astype(f.dtype)
    return jnp.einsum('blgc,gcd->blgd', spec, w_four).reshape(b, l, D_FOURIER)

def split_proj(proj):
    return jnp.split(proj, [D_SSD, D_SSD + CONV_DIM, D_SSD + CONV_DIM + 2 * SSD_HEADS], axis=-1)

def hier_moe(h, w_rg, b_rg, w_re, b_re, w_eg, w_eu, w_ed):
    bsz, l, d = h.shape
    t = h.reshape(bsz * l, d)
    n_tok = t.shape[0]
    f32 = jnp.float32
    p_grp = jax.nn.softmax((t @ w_rg + b_rg).astype(f32), axis=-1)
    p_top_grp, grp = lax.top_k(p_grp, 1)
    logit_exp = jnp.einsum('td,gde->tge', t, w_re) + b_re
    sel = jnp.broadcast_to(grp[:, :, None], (n_tok, 1, EXPERTS_PER_GROUP))
    logit_sel = jnp.take_along_axis(logit_exp, sel, axis=1)[:, 0]
    p_exp = jax.nn.softmax(logit_sel.astype(f32), axis=-1)
    p_top, j_top = lax.top_k(p_exp, TOP_K_INNER)
    gate = p_top_grp * p_top / jnp.sum(p_top, axis=-1, keepdims=True)
    eid = grp * EXPERTS_PER_GROUP + j_top
    n_assign = n_tok * TOP_K_INNER
    e_flat = eid.reshape(-1)
    g_flat = gate.reshape(-1)
    tok_flat = jnp.repeat(jnp.arange(n_tok, dtype=jnp.int32), TOP_K_INNER)
    order = jnp.argsort(e_flat)
    e_s, tok_s, g_s = e_flat[order], tok_flat[order], g_flat[order]
    counts = jnp.bincount(e_flat, length=N_EXPERTS)
    padded = (counts + EXPERT_BLOCK - 1) // EXPERT_BLOCK * EXPERT_BLOCK
    start = jnp.cumsum(counts) - counts
    end_pad = jnp.cumsum(padded)
    start_pad = end_pad - padded
    dest = start_pad[e_s] + jnp.arange(n_assign, dtype=jnp.int32) - start[e_s]
    n_blocks = -(-(n_assign + N_EXPERTS * (EXPERT_BLOCK - 1)) // EXPERT_BLOCK)
    n_rows = n_blocks * EXPERT_BLOCK
    row_tok = jnp.full((n_rows,), n_tok, jnp.int32).at[dest].set(tok_s)
    row_gate = jnp.zeros((n_rows,), f32).at[dest].set(g_s)
    blk_exp = jnp.minimum(jnp.searchsorted(end_pad, jnp.arange(n_blocks) * EXPERT_BLOCK, side='right'),
                          N_EXPERTS - 1)
    t_pad = jnp.concatenate([t, jnp.zeros((1, d), t.dtype)], axis=0)
    rows = t_pad[row_tok].reshape(n_blocks, EXPERT_BLOCK, d)

    def expert_block(args):
        xb, e = args
        return (jax.nn.silu(xb @ w_eg[e]) * (xb @ w_eu[e])) @ w_ed[e]

    y_rows = lax.map(expert_block, (rows, blk_exp)).reshape(n_rows, d)
    y = jax.ops.segment_sum(y_rows.astype(f32) * row_gate[:, None], row_tok,
                            num_segments=n_tok + 1)[:n_tok]
    return y.astype(h.dtype).reshape(bsz, l, d)

def second_inputs(seed: int = 0) -> dict:
    key = jax.random.key(seed)
    ks = jax.random.split(key, 26)
    f32 = jnp.float32

    def nrm(k, shape, scale):
        return jax.random.normal(k, shape, f32) * scale

    def gain(k, shape):
        return 1.0 + 0.05 * jax.random.normal(k, shape, f32)

    dt0 = jnp.exp(jax.random.uniform(ks[10], (DEPTH_2, 2, SSD_HEADS), f32,
                                     math.log(1e-3), math.log(1e-1)))
    dt_bias = dt0 + jnp.log(-jnp.expm1(-dt0))
    a_log = jnp.log(jax.random.uniform(ks[11], (DEPTH_2, 2, SSD_HEADS), f32, 1.0, 16.0))
    return {
        'x': nrm(ks[0], (BATCH, SEQ, D_MODEL), 1.0),
        'c': nrm(ks[1], (BATCH, D_MODEL), 1.0),
        'ctx': nrm(ks[2], (BATCH, CTX_LEN, D_MODEL), 1.0),
        'c_ctx': nrm(ks[3], (D_MODEL,), 1.0),
        'w_mod': nrm(ks[4], (DEPTH_2, D_MODEL, 6 * D_MODEL), D_MODEL ** -0.5),
        'b_mod': nrm(ks[5], (DEPTH_2, 6 * D_MODEL), 0.02),
        'norm1': gain(ks[6], (DEPTH_2, D_MODEL)),
        'w_in': nrm(ks[7], (DEPTH_2, D_MODEL, D_PROJ), D_MODEL ** -0.5),
        'conv_w': nrm(ks[8], (DEPTH_2, CONV_W, CONV_DIM), CONV_W ** -0.5),
        'conv_b': nrm(ks[9], (DEPTH_2, CONV_DIM), 0.02),
        'dt_bias': dt_bias,
        'a_log': a_log,
        'd_skip': gain(ks[12], (DEPTH_2, SSD_HEADS)),
        'ssd_norm': gain(ks[13], (DEPTH_2, D_SSD)),
        'w_four': nrm(ks[14], (DEPTH_2, FOURIER_GROUPS, FOURIER_CH, FOURIER_CH), FOURIER_CH ** -0.5),
        'w_out': nrm(ks[15], (DEPTH_2, D_MIX, D_MODEL), D_MIX ** -0.5),
        'norm2': gain(ks[16], (DEPTH_2, D_MODEL)),
        'w_rg': nrm(ks[17], (DEPTH_2, D_MODEL, N_EXPERT_GROUPS), D_MODEL ** -0.5),
        'b_rg': nrm(ks[18], (DEPTH_2, N_EXPERT_GROUPS), 0.01),
        'w_re': nrm(ks[19], (DEPTH_2, N_EXPERT_GROUPS, D_MODEL, EXPERTS_PER_GROUP), D_MODEL ** -0.5),
        'b_re': nrm(ks[20], (DEPTH_2, N_EXPERT_GROUPS, EXPERTS_PER_GROUP), 0.01),
        'w_eg': nrm(ks[21], (DEPTH_2, N_EXPERTS, D_MODEL, D_EXPERT), D_MODEL ** -0.5),
        'w_eu': nrm(ks[22], (DEPTH_2, N_EXPERTS, D_MODEL, D_EXPERT), D_MODEL ** -0.5),
        'w_ed': nrm(ks[23], (DEPTH_2, N_EXPERTS, D_EXPERT, D_MODEL), D_EXPERT ** -0.5),
        'final_norm': gain(ks[24], (D_MODEL,)),
    }

def second_block(x, c, ctx, c_ctx, w_mod, b_mod, norm1, w_in, conv_w, conv_b, dt_bias, a_log,
              d_skip, ssd_norm, w_four, w_out, norm2, w_rg, b_rg, w_re, b_re, w_eg, w_eu, w_ed,
              final_norm):
    n_lat = x.shape[1]
    rows = n_lat // GRID_W
    assert rows * GRID_W == n_lat
    bsz = x.shape[0]
    h_zero = jnp.zeros((bsz, SSD_GROUPS, SSD_HEADS_PER_GROUP, SSD_HEADDIM, SSD_STATE), jnp.float32)
    for layer in range(DEPTH_2):
        last = layer == DEPTH_2 - 1
        mod_lat = jax.nn.silu(c) @ w_mod[layer] + b_mod[layer]
        mod_ctx = jax.nn.silu(c_ctx) @ w_mod[layer] + b_mod[layer]
        sh1, sc1, g1, sh2, sc2, g2 = jnp.split(mod_lat[:, None, :], 6, axis=-1)
        sh1c, sc1c, g1c, sh2c, sc2c, g2c = jnp.split(mod_ctx, 6, axis=-1)
        prj_c = modulate(rmsnorm(ctx, norm1[layer]), sh1c, sc1c) @ w_in[layer]
        prj_l = modulate(rmsnorm(x, norm1[layer]), sh1, sc1) @ w_in[layer]
        z_c, xbc_c, dt_c, f_c = split_proj(prj_c)
        z_l, xbc_l, dt_l, f_l = split_proj(prj_l)
        y_c, hf_c, hb_c = ssd_mixer(z_c, xbc_c, dt_c, h_zero, h_zero, conv_w[layer], conv_b[layer],
                                    dt_bias[layer], a_log[layer], d_skip[layer], ssd_norm[layer])
        y_l, _, _ = ssd_mixer(z_l, xbc_l, dt_l, hf_c, hb_c, conv_w[layer], conv_b[layer],
                              dt_bias[layer], a_log[layer], d_skip[layer], ssd_norm[layer])
        mix_l = jnp.concatenate([y_l, fourier_mixer(f_l, w_four[layer])], axis=-1) @ w_out[layer]
        x = x + g1 * mix_l
        if not last:
            mix_c = jnp.concatenate([y_c, fourier_mixer(f_c, w_four[layer])], axis=-1) @ w_out[layer]
            ctx = ctx + g1c * mix_c
            ctx = ctx + g2c * hier_moe(modulate(rmsnorm(ctx, norm2[layer]), sh2c, sc2c), w_rg[layer],
                                       b_rg[layer], w_re[layer], b_re[layer], w_eg[layer],
                                       w_eu[layer], w_ed[layer])
        x = x + g2 * hier_moe(modulate(rmsnorm(x, norm2[layer]), sh2, sc2), w_rg[layer], b_rg[layer],
                              w_re[layer], b_re[layer], w_eg[layer], w_eu[layer], w_ed[layer])
    return rmsnorm(x, final_norm)


def setup_inputs(seed=0):
    out = dict(first_inputs(seed))
    for name, value in second_inputs(seed + 1).items():
        if name != "x":
            out[name + "_2"] = value
    return out


def reference(
    x, ret_w_in, ret_w_out, lru_w_in, lru_conv_w, lru_conv_b, lru_gate_w, lru_gate_b,
    lru_a_param, lru_w_out, norm_g, ffn_w_in, ffn_w_out, c_2, ctx_2, c_ctx_2, w_mod_2, b_mod_2,
    norm1_2, w_in_2, conv_w_2, conv_b_2, dt_bias_2, a_log_2, d_skip_2, ssd_norm_2, w_four_2,
    w_out_2, norm2_2, w_rg_2, b_rg_2, w_re_2, b_re_2, w_eg_2, w_eu_2, w_ed_2, final_norm_2,
):
    x = first_block(
        x, ret_w_in, ret_w_out, lru_w_in, lru_conv_w, lru_conv_b, lru_gate_w, lru_gate_b,
        lru_a_param, lru_w_out, norm_g, ffn_w_in, ffn_w_out,
    )
    return second_block(
        x, c_2, ctx_2, c_ctx_2, w_mod_2, b_mod_2, norm1_2, w_in_2, conv_w_2, conv_b_2,
        dt_bias_2, a_log_2, d_skip_2, ssd_norm_2, w_four_2, w_out_2, norm2_2, w_rg_2, b_rg_2,
        w_re_2, b_re_2, w_eg_2, w_eu_2, w_ed_2, final_norm_2,
    )


_drawn_inputs = setup_inputs


def setup_inputs(seed=0):
    import zlib

    import numpy as np

    out = dict(_drawn_inputs(seed))
    spreads = {}
    factors = {'lru_gate_b': 14.461,
     'ctx_2': 4.232,
     'norm1_2': 2.885,
     'conv_b_2': 8.0,
     'd_skip_2': 200.0,
     'ssd_norm_2': 3.546,
     'b_rg_2': 21.957,
     'b_re_2': 18.345,
     'norm2_2': 3.251}
    for name, (base, spread) in spreads.items():
        noise = np.random.default_rng([zlib.crc32(name.encode()), seed]).standard_normal(out[name].shape)
        drawn = base * np.exp(spread * noise) if base else spread * noise
        out[name] = jnp.asarray(drawn.astype(out[name].dtype))
    for name, factor in factors.items():
        out[name] = (out[name] * factor).astype(out[name].dtype)
    return out
```

```python
from contextlib import ExitStack

import numpy as np

import concourse.bass as bass
from concourse import mybir

F32 = mybir.dt.float32
F32R = mybir.dt.float32r
I32 = mybir.dt.int32
ALU = mybir.AluOpType
ACT = mybir.ActivationFunctionType
AX_X = mybir.AxisListType.X

P = 128
T = 256
D = 1024
KD = D // P
EPS = 1e-6

HEADS, DK, DV = 4, 256, 512
KV = HEADS * DV // P
LW = 1536
KL = LW // P
LCONV = 4
LPAD = LCONV - 1
FF = 2816
KF = FF // P
SH, SP_, SG_, SN = 16, 64, 4, 128
KX, KB = D // P, SG_ * SN // P
CONV = 5
CPAD = CONV // 2
ND = 2 * SH
FG = 4
NG, NJ, FE = 4, 8, 512
NE = NG * NJ
KE = FE // P
CAP = 64

UNIT = 4096
BPU = UNIT // P
BPC = 8
CHUNK = BPC * P
SPLIT = 3
RING = 6
ROT = 6
STAT, MODB = 6, 7

_VEC = [("norm_g", 8 * KD), ("lconv_w", LCONV * KL), ("lconv_b", KL), ("lgate_b", 2 * KL), ("a_param", KL),
        ("b_mod", 6 * KD), ("norm1", KD), ("conv_w", CONV * 16), ("conv_b", 16), ("d_skip", KD), ("ssd_norm", KD),
        ("norm2", KD), ("final", KD), ("c", 2 * KD), ("b_route", NG + NE), ("dt_bias", 1), ("a_log", 1),
        ("eps", 1), ("desc", NJ), ("forward", 1), ("backward", 1)]
VOFF, _n = {}, 0
for _name, _w in _VEC:
    VOFF[_name] = (_n, _w)
    _n += _w
NVEC = _n

STREAM = [("ret_g", 0, 4), ("ret_v", 0, 4), ("ret_q", 0, 2), ("ret_k", 0, 2), ("mod", 0, 1), ("ret_out", 0, 4),
          ("mod", 1, 2), ("ffn_in0", 0, 11), ("ffn_out0", 0, 6), ("mod", 3, 2), ("lru_u", 0, 3), ("lru_y", 0, 3),
          ("lru_gate", 0, 2), ("mod", 5, 3), ("lru_out", 0, 3), ("mod", 8, 2), ("ffn_in1", 0, 11),
          ("ffn_out1", 0, 6), ("mod", 10, 2), ("ssd_xs", 0, 2), ("ssd_b", 0, 1), ("ssd_c", 0, 1), ("ssd_z", 0, 2),
          ("ssd_f", 0, 1), ("mix_out", 0, 3)]
UNIT_AT, _n = {}, 0
for _name, _first, _count in STREAM:
    for _i in range(_count):
        UNIT_AT[_name, _first + _i] = _n + _i
    _n += _count
DENSE = _n

CHUNK_AT, _n = {}, 0
for _name, _blocks_of in (("ret_g", KV * KD), ("ret_v", KV * KD), ("ffn_in0", 2 * KF * KD), ("ffn_out0", KF * KD),
                          ("lru_u", KL * KD), ("lru_y", KL * KD), ("ffn_in1", 2 * KF * KD), ("ffn_out1", KF * KD)):
    CHUNK_AT[_name] = _n, _blocks_of // BPC
    _n += _blocks_of // BPC
CHUNK_UNIT = [(UNIT_AT[_name, _i * BPC // BPU], _i * BPC % BPU * P) for _name, (_f, _c) in CHUNK_AT.items()
              for _i in range(_c)]
EXPERT_UNITS = 3 * NE
BODY = 12


TILE, _seq = {}, []


def _tiles(name, n):
    _seq.extend((name, i) for i in range(n))


_tiles("g", 8)
_tiles("v", 8)
_tiles("q", 4)
_tiles("k", 4)
for _kind, _h in (("s", 0), ("s", 1), ("o", 0), ("s", 2), ("o", 1), ("t", 0), ("s", 3), ("o", 2), ("t", 1), ("o", 3),
                  ("t", 2), ("t", 3)):
    _tiles(f"{_kind}{_h}", 1 if _kind == "s" else 2)
_tiles("ret_out", 4)
_tiles("ffn_in0", 2 * KF // 2)
_tiles("ffn_out0", 4)
_tiles("lru_u", KL // 2)
_tiles("lru_y", KL // 2)
_tiles("lru_gate", KL)
_tiles("lru_out", 4)
_tiles("ffn_in1", 2 * KF // 2)
_tiles("ffn_out1", 4)
TURN_LAG = 3
for _m in range(KX + KB):
    _seq.append(("ssd_in", _m))
    if _m >= TURN_LAG:
        _seq.append(("turn", _m - TURN_LAG))
_tiles("ssd_dt", 1)
for _m in range(KB):
    _seq.append(("ssd_in", KX + KB + _m))
    if _m < TURN_LAG:
        _seq.append(("turn", KX + KB - TURN_LAG + _m))
_tiles("ssd_z", 4)
_tiles("ssd_f", 2)
_tiles("dt_tok", 1)
_tiles("state", SG_)


def head_order():
    yield "cb", 0
    yield "row", 0
    yield "row", 1
    for h in range(SH):
        if h + 2 < SH:
            if (h + 2) % 4 == 0:
                yield "cb", (h + 2) // 4
            yield "row", h + 2
        yield "y", h


for _kind, _i in head_order():
    if _kind != "y":
        _seq.append((_kind, _i))
    elif _i % 2 == 0:
        _seq.append(("y", _i // 2))
_tiles("dft", 3 * FG)
_tiles("mix_out", 4)
_tiles("t_tok", 4)
_tiles("route", 2)
for _n, _item in enumerate(_seq):
    TILE[_item] = _n


def two_blocks(nc, a, out):
    ctx = ExitStack()
    with ctx:
        def sb(name, shape, dt=F32):
            x = ctx.enter_context(nc.sbuf_tensor(name, shape, dt))
            base[name] = nc.sbuf_base - 4 * int(np.prod(shape[1:]))
            return x

        def over(of, off, name, *dims):
            return nc.alloc_sbuf_tensor_at(name, [P, *dims], F32R, offset=base[of] + 4 * off)

        def sem(name):
            return ctx.enter_context(nc.semaphore(name))

        ps = ctx.enter_context(nc.psum_tensor("ps", [P, 8, 512], F32))
        base = {}
        ring = [sb(f"ring{s}", [P, UNIT]) for s in range(RING)]
        X = sb("X", [P, KD, T])
        ones = sb("ones", [P, P])
        ident = sb("ident", [P, P])
        upper = sb("upper", [P, P])
        iota = sb("iota", [P, CAP])
        vec = sb("vec", [P, NVEC])
        cst = sb("cst", [P, 2560])
        lnb = sb("lnb", [P, T])
        rstd = sb("rstd", [P, T])
        mod = sb("mod", [P, 6 * KD, 2])
        coef = sb("coef", [P, 3, KD])
        csil = sb("csil", [P, KD, 2])
        act2 = sb("act2", [P, 2, 512])
        small = sb("small", [P, 640])
        rounds = sb("rounds", [P, 1], I32)
        a_lat = sb("a_lat", [ND, T])
        wdt = sb("wdt", [P, KD, ND])
        HM = sb("HM", [P, 2 * KD, T])
        SQ = sb("SQ", [P, KD, T])
        work = sb("work", [P, 13888])

        H, M = HM[:, 0:KD, :], HM[:, KD:2 * KD, :]
        flat_hm = HM[:, :, :].rearrange("p a b -> p (a b)")
        flat_sq = SQ[:, :, :].rearrange("p a b -> p (a b)")
        flat_cst = cst[:, :]

        def cut(v, *dims):
            if len(dims) == 1:
                return v
            if len(dims) == 2:
                return v.rearrange("p (a b) -> p a b", b=dims[1])
            return v.rearrange("p (a b c) -> p a b c", b=dims[1], c=dims[2])

        def at(off, *dims, of=None):
            return cut((work if of is None else of)[:, off:off + int(np.prod(dims))], *dims)

        def col(name, i=0, n=1, rows=P):
            return vec[0:rows, VOFF[name][0] + i:VOFF[name][0] + i + n]

        q, k, v, sg = at(0, HEADS * 2, T), at(2048, HEADS * 2, T), at(4096, 2, HEADS * DV), at(8192, KV, T)
        rope_tmp = at(2048, 2, 512, of=flat_hm)
        sT = at(3072, 2, 384, of=flat_hm)
        on = at(0, 4, 512, of=flat_sq)
        ost = at(0, 8, 6, of=small)
        omv = at(48, 8, 2, of=small)
        osd, ors = small[:, 64:72], small[:, 72:80]
        rcos, rsin = cst[:, 0:512], cst[:, 512:1024]
        decay = at(1024, HEADS, 384, of=flat_cst)
        in_hi, in_lo = over("HM", KD * T, "in_hi", KD, T), over("SQ", 0, "in_lo", KD, T)
        hid_hi, hid_lo = over("work", 0, "hid_hi", KF, T), over("work", KF * T, "hid_lo", KF, T)
        w_at = [("cst", 0), ("work", 2 * KF * T), ("HM", 0)]
        w_hi = [over(of, off, f"w_hi{n}", CHUNK) for n, (of, off) in enumerate(w_at)]
        w_lo = [over(of, off + CHUNK, f"w_lo{n}", CHUNK) for n, (of, off) in enumerate(w_at)]
        ret_hi = [over(of, off, f"ret_hi{n}", CHUNK) for n, (of, off) in enumerate((("work", 0), ("work", 2048), ("act2", 0)))]
        ret_lo = [over("work", off, f"ret_lo{n}", CHUNK) for n, off in enumerate((1024, 3072, 12288))]
        RET_CHUNKS = CHUNK_AT["ffn_in0"][0]

        def part_hi(n):
            return ret_hi[n % SPLIT] if n < RET_CHUNKS else w_hi[(n - RET_CHUNKS) % SPLIT]

        def part_lo(n):
            return ret_lo[n % SPLIT] if n < RET_CHUNKS else w_lo[(n - RET_CHUNKS) % SPLIT]

        upad, uc, gy, li = at(0, KL, LPAD + T), at(3108, KL, T), at(6180, KL, T), at(9252, KL, T)
        la = at(0, KL, T)
        lr_tail = at(12324, KL - KD, T)
        sp8, nsp8 = small[:, 96:96 + KL], small[:, 108:108 + KL]
        lsp = at(120, 3, KL, of=small)

        def r_tiles(i, n=1):
            return M[:, i:i + n, :] if i < KD else lr_tail[:, i - KD:i - KD + n, :]

        hcat = cut(flat_hm, KD, 2 * T)
        pad3 = at(0, 3, 2, T + 2 * CPAD)
        conv2 = at(1024, 2, 2, T, of=flat_sq)
        wctx = act2[:, :, 0:T]
        ctxT = at(1560, KD, T)
        xs_lat, b_lat, c_lat = at(1560, KX, T), at(3608, KB, T), at(4632, KB, T)
        xs_tok, b_tok = at(5656, 4, D), at(9752, 2, KB * P)
        mix = at(10776, KX + FG, T)
        h0 = at(0, SG_, 512, of=flat_sq)
        dtx, dta, dtb, dtc = (flat_sq[0:ND, 512 * i:512 * i + 512] for i in range(4))
        scr = flat_cst[0:ND, 2048:2560]
        wfour = at(2048, FG, P, of=flat_cst)
        elog, sneg, stot = small[0:ND, 161:162], small[0:ND, 160:161], small[0:ND, 162:163]
        tok6 = at(256, 6, ND, of=small)
        nega = at(448, 2, ND, of=small)
        xw = cut(flat_hm, 4, D)
        rmask, decm = at(0, 2, 2, 384, of=flat_hm), at(1536, 2, 2, 384, of=flat_hm)
        ce = at(3072, 2, 512, of=flat_hm)
        cbx = at(0, 2, 384)
        ccs = cst[:, 0:256]
        clx, slx = at(256, 2, T, of=flat_cst), at(768, 2, T, of=flat_cst)
        smask = at(1280, 2, 384, of=flat_cst)
        zz, spec = at(0, 2, 512, of=flat_hm), at(1024, 2, T, of=flat_hm)
        t_tok = cut(flat_hm[:, KD * T:2 * KD * T], 2, D)
        macc = SQ
        wroute = at(0, KD, NG + NE)
        logits = at(288, 2, NG + NE)
        posP, gateP = at(7360, NE // 2 + 1, 4), at(7428, NE // 2 + 1, 4)
        msk, gw, pos1 = at(512, 2, NE), at(576, 2, NE), at(640, 2, NE)
        rt = at(704, 24, 64)
        S2, SGb, SGt = at(2240, 2, T), at(2752, 2, T), at(3264, 2, T)
        xg = at(3776, KD, P)
        gs, hs, hT = at(4800, FE), at(5312, FE), at(6848, KE, P)
        yp = at(5824, D)

        slot_full = [sem(f"slot_full{i}") for i in range(RING)]
        slot_used = [sem(f"slot_used{i}") for i in range(RING)]
        bank_full = [sem(f"bank_full{i}") for i in range(ROT)]
        bank_read = [sem(f"bank_read{i}") for i in range(ROT)]
        s = {n: sem(n) for n in (
            "ld_x", "ld_vec", "ld_glob", "ld_ret", "ld_ssd", "ld_ctx", "ld_wdt", "ld_wfour", "ld_route",
            "ones_set", "csil_ready", "w_hi_ready", "w_lo_ready", "chunk_used", "in_hi_ready", "in_lo_ready",
            "sq_ready", "stats_full", "rstd_ready", "scaled_ready", "h_ready", "x_ready", "rope_done",
            "on_ready", "omv_ready", "osd_ready", "pads_zero", "uc_ready", "lsp_dve", "lsp_act", "a_ready",
            "th_ready", "lsq_arg", "lsq_ready", "go_ready", "mod_full", "mod_ready", "conv_ready", "wt_ready",
            "dt_dve", "dt_act", "dt_ready", "tok6_ready", "xw_ready", "ea_ready", "dec_ready",
            "m_ready", "even_head", "y_ready", "exp_arg", "exp_ready", "msk_ready", "route_ready", "moe_init",
            "eq_ready", "sel_ready", "gath_full", "xg_ready", "sc_full", "sc_free", "gu_full", "gs_ready",
            "hs_ready", "ht_full", "ht_ready", "y_full", "yp_ready", "out_done", "dve_step", "act_step")}

        def bank(t):
            return ps[:, t % ROT, :]

        def await_room(pe, t):
            if t >= ROT:
                pe.wait_ge(bank_read[t % ROT], t // ROT)

        def await_full(eng, t):
            eng.wait_ge(bank_full[t % ROT], t // ROT + 1)

        def await_read(eng, t):
            eng.wait_ge(bank_read[t % ROT], t // ROT + 1)

        def chunks_by(name, j):
            first, count = CHUNK_AT[name]
            if name == "ret_v":
                return min(first + 4 * (j + 1) + 2, first + count)
            blocks = 2 * (j + 1) * (KF if name.startswith("ffn_out") else KD)
            upto = first + -(-blocks // BPC) + 2
            return min(upto, first + count) if name.startswith("ffn_out") or name == "lru_y" else upto

        def rstd_of(n):
            return act2[:, 0, 0:T] if n == 9 else rstd[:, :]

        NORMS = [("h", 0), ("x", 0), ("h", 1), ("x", 1), ("h", 2), ("x", 2), ("h", 3), ("x", 3), ("h", 4), ("h", 5),
                 ("h", 6), ("h", 7), ("h", 8)]

        def await_norm(eng, n):
            kind, i = NORMS[n]
            eng.wait_ge(s["h_ready"] if kind == "h" else s["x_ready"], (KD if kind == "h" else 4) * (i + 1))

        block = ctx.enter_context(nc.Block())

        @block.sync
        def _(sp):
            sp.dma_start(vec[:, :], a["vec"]).then_inc(s["ld_vec"], 16)
            sp.dma_start(X[:, :, :], a["x"]).then_inc(s["ld_x"], 16)
            for u in range(DENSE):
                if u >= RING:
                    sp.wait_ge(slot_used[u % RING], u // RING)
                sp.dma_start(ring[u % RING][:, :], a["dense"][u]).then_inc(slot_full[u % RING], 16)

            def expert_round(r):
                with sp.Fori(0, EXPERT_UNITS // BODY) as b:
                    for j in range(BODY):
                        u = DENSE + j
                        sp.wait_ge(slot_used[u % RING], b * (BODY // RING) + r * (EXPERT_UNITS // RING) + u // RING)
                        sp.dma_start(ring[u % RING][:, :], a["experts"][bass.ds(b * BODY + j, 1)]
                                     .rearrange("u p n -> (u p) n")).then_inc(slot_full[u % RING], 16)

            expert_round(0)
            sp.wait_ge(s["route_ready"], 1)
            n_rounds = sp.value_load(rounds[0:1, 0:1], min_val=1, max_val=T // CAP)
            with sp.If(n_rounds > 1):
                with sp.Fori(1, n_rounds) as r:
                    expert_round(r)
            sp.wait_ge(s["h_ready"], KD * 9)
            sp.dma_start(out, H).then_inc(s["out_done"], 16)
            sp.wait_ge(s["out_done"], 16)

        @block.gpsimd
        def _(pool):
            pool.dma_start(cst[:, :], a["ret_cst"]).then_inc(s["ld_ret"], 16)
            pool.dma_start(iota[:, :], a["glob"][:, 0:CAP]).then_inc(s["ld_glob"], 16)
            pool.dma_start(ident[:, :], a["glob"][:, CAP:CAP + P]).then_inc(s["ld_glob"], 16)
            pool.dma_start(upper[:, :], a["glob"][:, CAP + P:CAP + 2 * P]).then_inc(s["ld_glob"], 16)
            pool.dma_start(wdt[:, :, :], a["wdt"]).then_inc(s["ld_wdt"], 16)
            await_read(pool, TILE["ffn_out1", 3])
            pool.dma_start(cst[:, 0:2048], a["ssd_cst"]).then_inc(s["ld_ssd"], 16)
            pool.dma_start(ctxT, a["ctx"]).then_inc(s["ld_ctx"], 16)
            pool.wait_ge(s["tok6_ready"], 1)
            pool.dma_start(wfour, a["wfour"]).then_inc(s["ld_wfour"], 16)
            pool.wait_ge(s["y_ready"], KX)
            pool.dma_start(wroute, a["wroute"]).then_inc(s["ld_route"], 16)

        @block.tensor
        def _(pe):
            left = []

            def weights(name, i):
                u = UNIT_AT[name, i]
                pe.wait_ge(slot_full[u % RING], 16 * (u // RING + 1))
                if 0 < u < DENSE - 1:
                    left.append(slot_used[(u - 1) % RING])
                return ring[u % RING]

            def mm(o, l, r, start, stop, inc=None):
                i = pe.matmul(o, l, r, start=start, stop=stop)
                if left:
                    assert inc is None
                    i.then_inc(left.pop(), 1)
                elif inc is not None:
                    i.then_inc(inc, 1)

            def gemm(name, tile, mtiles, ktiles, src, ready=None, cols=T, per=2, first_block=0, first_tile=0):
                for m in range(mtiles):
                    t = TILE[tile, first_tile + m // per]
                    if m % per == 0:
                        await_room(pe, t)
                    for c in range(ktiles):
                        b = first_block + m * ktiles + c
                        if b % BPU == 0:
                            gemm.w = weights(name, b // BPU)
                        if m == 0 and ready is not None:
                            ready(c)
                        last = c == ktiles - 1 and (m % per == per - 1 or m == mtiles - 1)
                        mm(bank(t)[:, (m % per) * cols:(m % per + 1) * cols], gemm.w[:, (b % BPU) * P:(b % BPU + 1) * P],
                           src(c), c == 0, c == ktiles - 1, bank_full[t % ROT] if last else None)

            def input_split(i):
                return lambda c: pe.wait_ge(s["in_lo_ready"], KD * i + c + 1)

            def split_gemm(name, mtiles, ktiles, hi, lo, ready=None, tile=None):
                for m in range(mtiles):
                    t = TILE[tile or name, m // 2]
                    if m % 2 == 0:
                        await_room(pe, t)
                    for c in range(ktiles):
                        b = m * ktiles + c
                        if b % BPU == 0:
                            weights(name, b // BPU)
                        n = CHUNK_AT[name][0] + b // BPC
                        if b % BPC == 0:
                            pe.wait_ge(s["w_lo_ready"], n + 1)
                            if n:
                                left.append(s["chunk_used"])
                        if m == 0 and ready is not None:
                            ready(c)
                        wh, wl = (w[:, b % BPC * P:(b % BPC + 1) * P] for w in (part_hi(n), part_lo(n)))
                        o = bank(t)[:, (m % 2) * T:(m % 2 + 1) * T]
                        mm(o, wh, hi[:, c, :], c == 0, False)
                        mm(o, wh, lo[:, c, :], False, False)
                        mm(o, wl, hi[:, c, :], False, c == ktiles - 1,
                           bank_full[t % ROT] if c == ktiles - 1 and m % 2 == 1 else None)

            def modulation(i):
                w = weights("mod", i)
                if i == 0:
                    pe.wait_ge(s["csil_ready"], 1)
                for m in range(4):
                    for c in range(KD):
                        b = m * KD + c
                        mm(ps[:, MODB, (4 * i + m) * 2:(4 * i + m) * 2 + 2], w[:, b * P:(b + 1) * P], csil[:, c, :],
                           c == 0, c == KD - 1, s["mod_full"] if m == 3 and c == KD - 1 else None)

            def norm_sums(squares):
                for j in range(4):
                    squares(j)
                    for c in (2 * j, 2 * j + 1):
                        mm(ps[:, STAT, 0:T], ones[:, :], SQ[:, c, :], c == 0, c == KD - 1,
                           s["stats_full"] if c == KD - 1 else None)

            def squares_of_input(i):
                return lambda j: pe.wait_ge(s["sq_ready"], 4 * i + j + 1)

            def squares_of_tiles(name):
                return lambda j: await_read(pe, TILE[name, j])

            def turned(t, srcs, last=True):
                for n, src in enumerate(srcs):
                    i = pe.transpose(bank(t)[:, n * P:(n + 1) * P], src, ident[:, :])
                i.then_inc(bank_full[t % ROT], 1)

            pe.wait_ge(s["ones_set"], 1)
            norm_sums(squares_of_input(0))

            split_gemm("ret_g", KV, KD, in_hi, in_lo, input_split(0), tile="g")
            for h in range(HEADS):
                t = TILE["v", 2 * h]
                await_room(pe, t)
                await_room(pe, t + 1)
                for c in range(KD):
                    if c == 0:
                        weights("ret_v", h)
                    n = CHUNK_AT["ret_v"][0] + 4 * h + c // 2
                    if c % 2 == 0:
                        pe.wait_ge(s["w_lo_ready"], n + 1)
                        left.append(s["chunk_used"])
                    wh, wl = (w[:, c % 2 * 512:(c % 2 + 1) * 512] for w in (part_hi(n), part_lo(n)))
                    for tau in range(2):
                        xh, xl = (x[:, c, tau * P:(tau + 1) * P] for x in (in_hi, in_lo))
                        mm(bank(t + tau), xh, wh, c == 0, False)
                        mm(bank(t + tau), xl, wh, False, False)
                        mm(bank(t + tau), xh, wl, False, c == KD - 1, bank_full[(t + tau) % ROT] if c == KD - 1 else None)
            gemm("ret_q", "q", 8, KD, lambda c: H[:, c, :])
            gemm("ret_k", "k", 8, KD, lambda c: H[:, c, :])

            def scores(h):
                t = TILE[f"s{h}", 0]
                await_room(pe, t)
                pe.wait_ge(s["rope_done"], 4 + h + 1)
                for c in range(2):
                    mm(bank(t)[:, 0:T], k[:, 2 * h + c, 0:P], q[:, 2 * h + c, :], c == 0, c == 1)
                for c in range(2):
                    mm(bank(t)[:, T:T + P], k[:, 2 * h + c, P:T], q[:, 2 * h + c, P:T], c == 0, c == 1,
                       bank_full[t % ROT] if c == 1 else None)

            def values(h):
                await_read(pe, TILE[f"s{h}", 0])
                await_read(pe, TILE["v", 2 * h + 1])
                t0, t1 = TILE[f"o{h}", 0], TILE[f"o{h}", 1]
                await_room(pe, t0)
                mm(bank(t0), sT[:, h % 2, 0:P], v[:, 0, h * DV:(h + 1) * DV], True, True, bank_full[t0 % ROT])
                await_room(pe, t1)
                mm(bank(t1), sT[:, h % 2, P:T], v[:, 0, h * DV:(h + 1) * DV], True, False)
                mm(bank(t1), sT[:, h % 2, T:T + P], v[:, 1, h * DV:(h + 1) * DV], False, True, bank_full[t1 % ROT])

            def turn_head(h):
                for tau in range(2):
                    t = TILE[f"t{h}", tau]
                    await_room(pe, t)
                    await_read(pe, TILE[f"o{h}", tau])
                    turned(t, [on[:, (2 * h + tau) % 4, c * P:(c + 1) * P] for c in range(4)])

            pe.wait_ge(s["ld_glob"], 48)
            for step, h in ((scores, 0), (scores, 1), (values, 0), (scores, 2), (values, 1), (turn_head, 0), (scores, 3),
                            (values, 2), (turn_head, 1), (values, 3), (modulation, 0), (turn_head, 2), (turn_head, 3)):
                step(h)
            for tau in range(2):
                for h in range(HEADS):
                    await_read(pe, TILE[f"t{h}", tau])
            gemm("ret_out", "ret_out", KD, KV, lambda c: sg[:, c, :])
            norm_sums(squares_of_tiles("ret_out"))
            modulation(1)
            norm_sums(squares_of_input(1))
            modulation(2)

            def ffn(layer):
                split_gemm(f"ffn_in{layer}", 2 * KF, KD, in_hi, in_lo,
                           input_split(2 * layer + 1))
                split_gemm(f"ffn_out{layer}", KD, KF, hid_hi, hid_lo,
                           lambda c: await_read(pe, TILE[f"ffn_in{layer}", c // 2 * 2 + 1]))

            ffn(0)
            norm_sums(squares_of_tiles("ffn_out0"))
            modulation(3)
            norm_sums(squares_of_input(2))
            modulation(4)

            split_gemm("lru_u", KL, KD, in_hi, in_lo, input_split(2))
            split_gemm("lru_y", KL, KD, in_hi, in_lo)
            for n in range(KL // 2):
                if n % 3 == 0:
                    w = weights("lru_gate", n // 3)
                pe.wait_ge(s["uc_ready"], 2 * n + 2)
                for gate in range(2):
                    t = TILE["lru_gate", 2 * n + gate]
                    await_room(pe, t)
                    for m in range(2):
                        for c in range(2):
                            b = ((n % 3) * 2 + gate) * 4 + m * 2 + c
                            mm(bank(t)[:, m * T:(m + 1) * T], w[:, b * P:(b + 1) * P], uc[:, 2 * n + c, :], c == 0,
                               c == 1, bank_full[t % ROT] if m == 1 and c == 1 else None)
            for i in range(5, 8):
                modulation(i)
            gemm("lru_out", "lru_out", KD, KL, lambda c: li[:, c, :], lambda c: pe.wait_ge(s["go_ready"], c // 4 + 1))
            norm_sums(squares_of_tiles("lru_out"))
            modulation(8)
            norm_sums(squares_of_input(3))
            modulation(9)
            ffn(1)
            norm_sums(squares_of_tiles("ffn_out1"))
            modulation(10)
            modulation(11)
            norm_sums(squares_of_input(4))
            norm_sums(squares_of_input(5))

            def turn(m):
                pe.wait_ge(s["wt_ready"], m + 1)
                t = TILE["turn", m]
                await_room(pe, t)
                blocks = [wctx[:, m % 2, 0:P], wctx[:, m % 2, P:T]]
                if m < KX:
                    blocks += [xs_lat[:, m, 0:P], xs_lat[:, m, P:T]]
                turned(t, blocks)

            for m in range(KX + KB):
                name, i = ("ssd_xs", m) if m < KX else ("ssd_b", m - KX)
                gemm(name, "ssd_in", 1, KD, lambda c: hcat[:, c, :],
                     (lambda c: pe.wait_ge(s["h_ready"], KD * 5 + c + 1)) if m == 0 else None, cols=2 * T, per=1,
                     first_block=i * KD, first_tile=m)
                if m >= TURN_LAG:
                    turn(m - TURN_LAG)
            t = TILE["ssd_dt", 0]
            await_room(pe, t)
            pe.wait_ge(s["ld_wdt"], 16)
            for c in range(KD):
                mm(bank(t)[0:ND, :], wdt[:, c, :], hcat[:, c, :], c == 0, c == KD - 1,
                   bank_full[t % ROT] if c == KD - 1 else None)
            for m in range(KB):
                gemm("ssd_c", "ssd_in", 1, KD, lambda c: hcat[:, c, T:2 * T], per=1, first_block=m * KD,
                     first_tile=KX + KB + m)
                if m < TURN_LAG:
                    turn(KX + KB - TURN_LAG + m)
            gemm("ssd_z", "ssd_z", KX, KD, lambda c: hcat[:, c, T:2 * T])
            gemm("ssd_f", "ssd_f", FG, KD, lambda c: hcat[:, c, T:2 * T])
            t = TILE["dt_tok", 0]
            await_room(pe, t)
            pe.wait_ge(s["dt_ready"], 1)
            for n, src in enumerate((a_lat[:, 0:P], a_lat[:, P:T], dtx[:, T:T + P], dtx[:, T + P:2 * T],
                                     dtx[:, 0:P], dtx[:, P:T])):
                i = pe.transpose(bank(t)[:, n * ND:(n + 1) * ND], src, ident[0:ND, 0:ND])
            i.then_inc(bank_full[t % ROT], 1)
            pe.wait_ge(s["xw_ready"], 4)
            await_read(pe, TILE["turn", KX + KB - 1])
            await_read(pe, TILE["turn", KX + KB - 2])
            for g in range(SG_):
                t = TILE["state", g]
                await_room(pe, t)
                for d in range(2):
                    for tau in range(2):
                        mm(bank(t)[:, d * 256:(d + 1) * 256], b_tok[:, tau, g * P:(g + 1) * P],
                           xw[:, 2 * d + tau, g * 256:(g + 1) * 256], tau == 0, tau == 1,
                           bank_full[t % ROT] if d == 1 and tau == 1 else None)
            pe.wait_ge(s["wt_ready"], KX + 2 * KB)
            for kind, i in head_order():
                if kind == "cb":
                    t = TILE["cb", i]
                    await_room(pe, t)
                    for j in range(2):
                        mm(bank(t)[:, j * T:(j + 1) * T], b_lat[:, i, j * P:(j + 1) * P], c_lat[:, i, :], True, True,
                           bank_full[t % ROT] if j == 1 else None)
                elif kind == "row":
                    t = TILE["row", i]
                    await_room(pe, t)
                    for d in range(2):
                        n = d * SH + i
                        mm(bank(t)[:, d * T:(d + 1) * T], ident[0:ND, n:n + 1].to_broadcast([ND, P]), a_lat[:, :], True,
                           True, bank_full[t % ROT] if d == 1 else None)
                else:
                    t = TILE["y", i // 2]
                    if i % 2 == 0:
                        await_room(pe, t)
                    if i == 0:
                        await_read(pe, TILE["state", 2])
                        await_read(pe, TILE["state", 3])
                    pe.wait_ge(s["m_ready"], i + 1)
                    rows = slice((i % 2) * SP_, (i % 2 + 1) * SP_)
                    xh = [xs_tok[:, 2 + j, i * SP_:(i + 1) * SP_] for j in range(2)]
                    dm, par = decm[:, i % 2], i % 2
                    state_of = h0[:, i // 4, :]
                    lo = (i % 4) * SP_
                    mm(bank(t)[rows, 0:T], xh[0], dm[:, 0, 0:T], True, False)
                    mm(bank(t)[rows, 0:P], xh[0], dm[:, 0, T:T + P], False, False)
                    mm(bank(t)[rows, P:T], xh[1], dm[:, 1, 0:P], False, False)
                    mm(bank(t)[rows, 0:T], xh[1], dm[:, 1, P:P + T], False, False)
                    mm(bank(t)[rows, 0:T], state_of[:, lo:lo + SP_], ce[:, par, 0:T], False, False)
                    mm(bank(t)[rows, 0:T], state_of[:, 256 + lo:256 + lo + SP_], ce[:, par, T:2 * T], False, True,
                       bank_full[t % ROT] if i % 2 == 1 else s["even_head"])

            def fourier(g):
                t = TILE["dft", 3 * g]
                await_room(pe, t)
                if g == 0:
                    await_read(pe, TILE["ssd_f", 1])
                    pe.wait_ge(s["ld_wfour"], 16)
                for tau in range(2):
                    mm(bank(t)[:, tau * 256:(tau + 1) * 256], mix[:, KX + g, tau * P:(tau + 1) * P], ccs, True, True,
                       bank_full[t % ROT] if tau == 1 else None)
                await_room(pe, t + 1)
                await_read(pe, t)
                for n, (tau, part, tab) in enumerate(((0, 0, clx), (1, 0, clx), (0, 1, slx), (1, 1, slx))):
                    lo = tau * 256 + part * P
                    mm(bank(t + 1)[:, 0:T], zz[:, g % 2, lo:lo + P], tab[:, tau, :], n == 0, n == 3,
                       bank_full[(t + 1) % ROT] if n == 3 else None)
                await_room(pe, t + 2)
                await_read(pe, t + 1)
                mm(bank(t + 2)[:, 0:T], wfour[:, g, :], spec[:, g % 2, :], True, True, bank_full[(t + 2) % ROT])

            fourier(0)
            norm_sums(squares_of_input(6))
            for g in range(1, FG):
                fourier(g)
            gemm("mix_out", "mix_out", KD, KX + FG, lambda c: mix[:, c, :],
                 lambda c: pe.wait_ge(s["h_ready"], KD * 6 + c + 1) if c < KX else await_read(pe, TILE["dft", 3 * (c - KX) + 2]))
            norm_sums(squares_of_input(7))

            pe.wait_ge(s["ld_route"], 16)
            pe.wait_ge(s["h_ready"], KD * 8)
            t = TILE["route", 0]
            for tau in range(2):
                for half in range(2):
                    tt = TILE["t_tok", 2 * tau + half]
                    await_room(pe, tt)
                    turned(tt, [H[:, 4 * half + c, tau * P:(tau + 1) * P] for c in range(4)])
            await_room(pe, t)
            for tau in range(2):
                for c in range(KD):
                    mm(bank(t)[:, tau * 64:tau * 64 + NG + NE], H[:, c, tau * P:(tau + 1) * P], wroute[:, c, :],
                       c == 0, c == KD - 1, bank_full[t % ROT] if tau == 1 and c == KD - 1 else None)
            t = TILE["route", 1]
            await_room(pe, t)
            pe.wait_ge(s["msk_ready"], 1)
            mm(bank(t)[:, 0:NE], upper[:, :], msk[:, 0, :], True, True)
            mm(bank(t)[:, NE:2 * NE], ones[:, :], msk[:, 0, :], True, False)
            mm(bank(t)[:, NE:2 * NE], upper[:, :], msk[:, 1, :], False, True)
            mm(bank(t)[:, 2 * NE:3 * NE], ones[:, :], msk[:, 0, :], True, False)
            mm(bank(t)[:, 2 * NE:3 * NE], ones[:, :], msk[:, 1, :], False, True, bank_full[t % ROT])

            for j in range(4):
                await_read(pe, TILE["t_tok", j])
            pe.wait_ge(s["route_ready"], 1)
            pe.wait_ge(s["moe_init"], 1)
            n_rounds = pe.value_load(rounds[0:1, 0:1], min_val=1, max_val=T // CAP)

            def scatter(use0, n0, par):
                for part in range(4):
                    pe.wait_ge(s["sc_free"], use0 + (n0 + max(part, 1) + 1))
                    for m in range(2):
                        c = 2 * part + m
                        i = pe.matmul(ps[:, 6 + (n0 + part) % 2, m * T:(m + 1) * T], yp[:, c * P:(c + 1) * P],
                                      SGt[:, par, :], start=True, stop=True)
                    i.then_inc(s["sc_full"], 1)

            def gather(par, count):
                pe.wait_ge(s["sel_ready"], count)
                for c in range(KD):
                    for tau in range(2):
                        i = pe.matmul(ps[:, 2 + c // 4, (c % 4) * P:(c % 4 + 1) * P],
                                      t_tok[:, tau, c * P:(c + 1) * P], S2[:, par, tau * P:(tau + 1) * P],
                                      start=tau == 0, stop=tau == 1)
                i.then_inc(s["gath_full"], 1)

            gather(0, 1)
            with pe.Fori(0, n_rounds) as r:
                with pe.Fori(0, EXPERT_UNITS // BODY) as b:
                    turns = r * (EXPERT_UNITS // BODY) + b
                    for par in range(2):
                        pair = turns * 2 + par

                        def expert_weights(j):
                            u = DENSE + 6 * par + j
                            pe.wait_ge(slot_full[u % RING], turns * (16 * BODY // RING) + 16 * (u // RING + 1))
                            left.append(slot_used[(u - 2) % RING])
                            return ring[u % RING]

                        pe.wait_ge(s["xg_ready"], pair * 2 + 2)
                        for up in range(2):
                            if up:
                                pe.wait_ge(s["yp_ready"], pair + 1)
                                scatter(turns * 10, 5 * par, 1 - par)
                            w = expert_weights(2 * up), expert_weights(2 * up + 1)
                            for c in range(KD):
                                for e in range(2):
                                    mm(ps[e * CAP:(e + 1) * CAP, up, :], xg[:, c, e * CAP:(e + 1) * CAP],
                                       w[e][:, c * FE:(c + 1) * FE], c == 0, c == KD - 1,
                                       s["gu_full"] if e == 1 and c == KD - 1 else None)
                        pe.wait_ge(s["sc_free"], turns * 10 + (5 * par + 5))
                        for tau in range(2):
                            i = pe.transpose(ps[:, 6 + (5 * par + 4) % 2, tau * P:(tau + 1) * P],
                                             SGb[:, par, tau * P:(tau + 1) * P], ident[:, :])
                        i.then_inc(s["sc_full"], 1)
                        gather(1 - par, pair + 2)
                        pe.wait_ge(s["hs_ready"], pair + 1)
                        for c in range(KE):
                            i = pe.transpose(ps[:, 0, c * P:(c + 1) * P], hs[:, c * P:(c + 1) * P], ident[:, :])
                        i.then_inc(s["ht_full"], 1)
                        pe.wait_ge(s["ht_ready"], pair + 1)
                        w = expert_weights(4), expert_weights(5)
                        for c in range(KE):
                            for half in range(2):
                                for e in range(2):
                                    lo = c * D + half * 512
                                    mm(ps[e * CAP:(e + 1) * CAP, 4 + half, :], hT[:, c, e * CAP:(e + 1) * CAP],
                                       w[e][:, lo:lo + 512], c == 0, c == KE - 1,
                                       s["y_full"] if e == 1 and c == KE - 1 and half == 1 else None)
            pe.wait_ge(s["yp_ready"], n_rounds * (NE // 2) + 1)
            scatter(n_rounds * (5 * NE // 2), 0, 1)
            norm_sums(squares_of_input(8))

        @block.scalar
        def _(act):
            steps = [0]

            def fn(o, i, f, inc=None, **kw):
                x = act.activation(o, i, f, **kw)
                if inc is not None:
                    x.then_inc(inc, 1)
                return x

            def settle(x):
                x.then_inc(s["act_step"], 1)
                steps[0] += 1
                act.wait_ge(s["act_step"], steps[0])

            def read(t, o, f=ACT.Copy, cols=512, **kw):
                await_full(act, t)
                fn(o, bank(t)[:, 0:cols], f, bank_read[t % ROT], **kw)

            def pairs(v, j):
                return v[:, 2 * j:2 * j + 2, :].rearrange("p a b -> p (a b)")

            def squares(src, ready):
                for j in range(4):
                    ready(j)
                    fn(pairs(SQ, j), pairs(src, j), ACT.Square, s["sq_ready"])

            def inv_rms(n):
                act.wait_ge(s["stats_full"], n + 1)
                if n and n != 9:
                    await_norm(act, n - 1)
                settle(fn(lnb[:, :], ps[:, STAT, 0:T], ACT.Ln, scale=1.0 / D, bias=col("eps")))
                fn(rstd_of(n), lnb[:, :], ACT.Exp, s["rstd_ready"], scale=-0.5)

            def modulated(k, dst, gain, shift):
                for c in range(KD):
                    act.wait_ge(s["scaled_ready"], KD * k + c + 1)
                    fn(dst(c), dst(c), ACT.Identity, s["h_ready"], scale=gain(c), bias=shift(c))

            def mixer_out(name, before=None):
                for j in range(4):
                    t = TILE[name, j]
                    if before is not None:
                        before(j)
                    await_full(act, t)
                    fn(pairs(M, j), bank(t), ACT.Copy)
                    fn(pairs(SQ, j), bank(t), ACT.Square, bank_read[t % ROT])

            def x_after(i):
                return lambda j: act.wait_ge(s["x_ready"], 4 * i + j + 1)

            chunk = [0]

            def weights_hi(upto):
                for n in range(chunk[0], upto):
                    u, lo = CHUNK_UNIT[n]
                    act.wait_ge(slot_full[u % RING], 16 * (u // RING + 1))
                    if n >= SPLIT:
                        act.wait_ge(s["chunk_used"], n - SPLIT + 1)
                    fn(part_hi(n)[:, :], ring[u % RING][:, lo:lo + CHUNK], ACT.Copy, s["w_hi_ready"])
                chunk[0] = max(chunk[0], upto)

            def input_hi(i):
                for c in range(KD):
                    act.wait_ge(s["h_ready"], KD * i + c + 1)
                    fn(in_hi[:, c, :], H[:, c, :], ACT.Copy, s["in_hi_ready"])
                act.wait_ge(s["in_lo_ready"], KD * (i + 1))

            act.wait_ge(s["ld_vec"], 16)
            fn(csil[:, :, :].rearrange("p a b -> p (a b)"), col("c", 0, 2 * KD), ACT.Silu, s["csil_ready"])
            act.wait_ge(s["ld_x"], 16)
            squares(X, lambda j: None)
            inv_rms(0)
            weights_hi(1)
            input_hi(0)
            for j in range(8):
                weights_hi(chunks_by("ret_g", j))
                read(TILE["g", j], pairs(sg, j), ACT.Silu)
            for j in range(8):
                h, tau = divmod(j, 2)
                weights_hi(chunks_by("ret_v", h))
                read(TILE["v", j], v[:, tau, h * DV:(h + 1) * DV])
            act.wait_ge(s["lsp_dve"], 1)
            fn(lsp[:, 0, :], lsp[:, 0, :], ACT.Exp, s["lsp_act"], scale=-1.0)
            act.wait_ge(s["lsp_dve"], 2)
            fn(lsp[:, 2, :], lsp[:, 1, :], ACT.Ln, s["lsp_act"])
            for j in range(2 * HEADS):
                act.wait_ge(s["omv_ready"], j + 1)
                fn(osd[:, j:j + 1], omv[:, j, 1:2], ACT.Sqrt, s["osd_ready"], bias=col("eps"))
            mixer_out("ret_out")
            inv_rms(1)
            squares(X, x_after(0))
            weights_hi(CHUNK_AT["ffn_in0"][0] + 2)
            inv_rms(2)

            def ffn(layer, i):
                input_hi(i)
                for j in range(KF // 2):
                    tg, tu = TILE[f"ffn_in{layer}", 2 * j], TILE[f"ffn_in{layer}", 2 * j + 1]
                    weights_hi(chunks_by(f"ffn_in{layer}", 2 * j))
                    if j >= 2:
                        await_read(act, tu - 4)
                    read(tg, act2[:, j % 2, :], ACT.Silu)
                mixer_out(f"ffn_out{layer}", lambda j: weights_hi(chunks_by(f"ffn_out{layer}", j)))

            ffn(0, 1)
            inv_rms(3)
            squares(X, x_after(1))
            weights_hi(CHUNK_AT["lru_u"][0] + 2)
            inv_rms(4)
            input_hi(2)
            act.wait_ge(s["pads_zero"], 1)
            for j in range(KL // 2):
                t = TILE["lru_u", j]
                weights_hi(chunks_by("lru_u", j))
                await_full(act, t)
                fn(upad[:, 2 * j:2 * j + 2, LPAD:], cut(bank(t), 2, T), ACT.Copy, bank_read[t % ROT])
            for j in range(KL // 2):
                weights_hi(chunks_by("lru_y", j))
                read(TILE["lru_y", j], pairs(gy, j), ACT.Gelu_apprx_tanh)
            for n in range(KL // 2):
                for gate in range(2):
                    t = TILE["lru_gate", 2 * n + gate]
                    await_full(act, t)
                    for m in range(2):
                        i = 2 * n + m
                        o = (r_tiles(i) if gate == 0 else li[:, i:i + 1, :]).rearrange("p a b -> p (a b)")
                        fn(o, bank(t)[:, m * T:(m + 1) * T], ACT.Sigmoid, bank_read[t % ROT] if m == 1 else None,
                           bias=col("lgate_b", gate * KL + i))
            act.wait_ge(s["lsp_dve"], 3)
            for n in range(3):
                for i in range(4 * n, 4 * n + 4):
                    if i == 0:
                        await_read(act, TILE["lru_gate", KL - 1])
                        await_read(act, TILE["lru_gate", KL - 2])
                    fn(la[:, i, :], r_tiles(i)[:, 0, :], ACT.Exp, s["a_ready"] if i % 4 == 3 else None,
                       scale=nsp8[:, i:i + 1])
            for n in range(3):
                act.wait_ge(s["a_ready"], n + 1)
                for i in range(4 * n, 4 * n + 4):
                    fn(r_tiles(i)[:, 0, :], r_tiles(i)[:, 0, :], ACT.Tanh, s["th_ready"] if i % 4 == 3 else None,
                       scale=sp8[:, i:i + 1])
            for n in range(3):
                act.wait_ge(s["lsq_arg"], n + 1)
                u4 = uc[:, 4 * n:4 * n + 4, :].rearrange("p a b -> p (a b)")
                fn(u4, u4, ACT.Sqrt, s["lsq_ready"])
            mixer_out("lru_out")
            inv_rms(5)
            squares(X, x_after(2))
            weights_hi(CHUNK_AT["ffn_in1"][0] + 2)
            inv_rms(6)
            ffn(1, 3)
            inv_rms(7)
            act.wait_ge(s["ld_ctx"], 16)
            squares(ctxT, lambda j: None)
            inv_rms(8)
            squares(X, x_after(3))
            inv_rms(9)
            modulated(0, lambda c: hcat[:, c, 0:T], lambda c: coef[:, 0, c:c + 1], lambda c: mod[:, c, 1:2])
            modulated(1, lambda c: hcat[:, c, T:2 * T], lambda c: coef[:, 1, c:c + 1], lambda c: mod[:, c, 0:1])
            act.wait_ge(s["pads_zero"], 2)

            def padded(m):
                t = TILE["ssd_in", m]
                await_full(act, t)
                if m >= 3:
                    act.wait_ge(s["conv_ready"], m - 2)
                if m < KX + KB:
                    fn(pad3[:, m % 3, :, CPAD:CPAD + T], cut(bank(t), 2, T), ACT.Copy, bank_read[t % ROT])
                else:
                    fn(pad3[:, m % 3, 1, CPAD:CPAD + T], bank(t)[:, 0:T], ACT.Copy, bank_read[t % ROT])

            def silu_tile(m):
                act.wait_ge(s["conv_ready"], m + 1)
                o = xs_lat[:, m, :] if m < KX else b_lat[:, m - KX, :] if m < KX + KB else c_lat[:, m - KX - KB, :]
                if m < KX + KB:
                    fn(wctx[:, m % 2, :], conv2[:, m % 2, 0, :], ACT.Silu)
                fn(o, conv2[:, m % 2, 1, :], ACT.Silu, s["wt_ready"])

            def turned_tile(m):
                t = TILE["turn", m]
                await_full(act, t)
                if m < KX:
                    fn(xs_tok[:, :, m * P:(m + 1) * P], cut(bank(t), 4, P), ACT.Copy, bank_read[t % ROT])
                else:
                    g = m - KX
                    fn(b_tok[:, :, g * P:(g + 1) * P], cut(bank(t)[:, 0:T], 2, P), ACT.Copy, bank_read[t % ROT])

            for m in range(KX + KB):
                padded(m)
                if m >= TURN_LAG:
                    turned_tile(m - TURN_LAG)
                if m >= 1:
                    silu_tile(m - 1)
            for m in range(KB):
                padded(KX + KB + m)
                if m < TURN_LAG:
                    turned_tile(KX + KB - TURN_LAG + m)
                silu_tile(KX + KB + m - 1)
            silu_tile(KX + 2 * KB - 1)
            act.wait_ge(s["dt_dve"], 1)
            fn(dtb, dtb, ACT.Exp, s["dt_act"], scale=-1.0)
            fn(elog, col("a_log", rows=ND), ACT.Exp, s["dt_act"])
            act.wait_ge(s["dt_dve"], 2)
            fn(dta, dtc, ACT.Ln, s["dt_act"])
            act.wait_ge(s["dt_dve"], 3)
            fn(dtc[:, 0:T], dtc[:, 0:T], ACT.Exp, s["dt_act"])
            for j in range(4):
                read(TILE["ssd_z", j], pairs(mix, j), ACT.Silu)
            for j in range(2):
                read(TILE["ssd_f", j], pairs(mix, 4 + j))
            for g in range(SG_):
                read(TILE["state", g], h0[:, g, :])
            act.wait_ge(s["tok6_ready"], 1)
            for h in range(SH):
                t = TILE["row", h]
                await_full(act, t)
                if h >= 2:
                    act.wait_ge(s["m_ready"], h - 1)
                fn(act2[:, h % 2, :], bank(t), ACT.Exp, s["ea_ready"])
                await_read(act, t)
                if h >= 2:
                    if h % 2 == 0:
                        act.wait_ge(s["even_head"], h // 2)
                    else:
                        await_full(act, TILE["y", (h - 2) // 2])
                dm, rm = decm[:, h % 2], rmask[:, h % 2]
                for j in range(2):
                    mid = T - j * P
                    fn(dm[:, j, 0:mid], rm[:, j, 0:mid], ACT.Exp, bias=nega[:, j, h:h + 1])
                    fn(dm[:, j, mid:384], rm[:, j, mid:384], ACT.Exp, s["dec_ready"] if j == 1 else None,
                       bias=nega[:, j, SH + h:SH + h + 1])
            squares(xs_lat, lambda j: act.wait_ge(s["y_ready"], KX))

            def fourier(g):
                t = TILE["dft", 3 * g]
                read(t, zz[:, g % 2, :])
                read(t + 1, spec[:, g % 2, :], cols=T)
                read(t + 2, mix[:, KX + g, :], cols=T)

            fourier(0)
            inv_rms(10)
            for g in range(1, FG):
                fourier(g)
            squares(X, lambda j: await_read(act, TILE["mix_out", j]))
            inv_rms(11)
            modulated(2, lambda c: H[:, c, :], lambda c: coef[:, 2, c:c + 1], lambda c: mod[:, 3 * KD + c, 0:1])
            for tau in range(2):
                for half in range(2):
                    read(TILE["t_tok", 2 * tau + half], t_tok[:, tau, half * 512:(half + 1) * 512])
            act.wait_ge(s["exp_arg"], 1)
            fn(rt[:, 1, 0:8], rt[:, 0, 0:8], ACT.Exp, s["exp_ready"])
            act.wait_ge(s["exp_arg"], 2)
            fn(rt[:, 14, 0:2], rt[:, 13, 0:2], ACT.Exp, s["exp_ready"])
            act.wait_ge(s["route_ready"], 1)
            n_rounds = act.value_load(rounds[0:1, 0:1], min_val=1, max_val=T // CAP)

            def gathered(count):
                act.wait_ge(s["gath_full"], count)
                for half in range(2):
                    fn(xg[:, 4 * half:4 * half + 4, :].rearrange("p a b -> p (a b)"), ps[:, 2 + half, :], ACT.Copy,
                       s["xg_ready"])

            gathered(1)
            with act.Fori(0, n_rounds) as r:
                with act.Fori(0, EXPERT_UNITS // BODY) as b:
                    for par in range(2):
                        pair = r * (NE // 2) + b * 2 + par
                        act.wait_ge(s["gu_full"], pair * 2 + 1)
                        fn(gs, ps[:, 0, :], ACT.Silu, s["gs_ready"])
                        act.wait_ge(s["ht_full"], pair + 1)
                        fn(hT[:, :, :].rearrange("p a b -> p (a b)"), ps[:, 0, :], ACT.Copy, s["ht_ready"])
                        gathered(pair + 2)
                        act.wait_ge(s["y_full"], pair + 1)
                        fn(yp, ps[:, 4:6, :].rearrange("p a b -> p (a b)"), ACT.Copy, s["yp_ready"])
            squares(X, x_after(4))
            inv_rms(12)

        @block.vector
        def _(dve):
            steps = [0]

            def settle(x):
                x.then_inc(s["dve_step"], 1)
                steps[0] += 1
                dve.wait_ge(s["dve_step"], steps[0])

            def tt(o, x, y, op, inc=None):
                i = dve.tensor_tensor(out=o, in0=x, in1=y, op=op)
                if inc is not None:
                    i.then_inc(inc, 1)
                return i

            def ts(o, x, s1, op0, s2=None, op1=None, inc=None):
                i = dve.tensor_scalar(o, x, s1, s2, op0, op1) if op1 is not None else dve.tensor_scalar(o, x, s1, None, op0)
                if inc is not None:
                    i.then_inc(inc, 1)
                return i

            def stt(o, x, sc, y, op0, op1, inc=None):
                i = dve.scalar_tensor_tensor(out=o, in0=x, scalar=sc, in1=y, op0=op0, op1=op1)
                if inc is not None:
                    i.then_inc(inc, 1)
                return i

            MUL, ADD, SUB, MAX, EQ = ALU.mult, ALU.add, ALU.subtract, ALU.max, ALU.is_equal

            def log1p_end(e, w, l, x, o):
                settle(ts(w, w, 1.0, SUB))
                settle(stt(o, w, 0.0, w, EQ, ADD))
                settle(dve.reciprocal(o, o))
                settle(tt(o, o, e, MUL))
                settle(tt(o, o, l, MUL))
                settle(stt(w, w, 0.0, e, EQ, MUL))
                settle(tt(o, o, w, ADD))
                settle(stt(o, x, 0.0, o, MAX, ADD))

            chunk = [0]

            def weights_lo(upto):
                for n in range(chunk[0], upto):
                    u, lo = CHUNK_UNIT[n]
                    dve.wait_ge(s["w_hi_ready"], n + 1)
                    tt(part_lo(n)[:, :], ring[u % RING][:, lo:lo + CHUNK], part_hi(n)[:, :].bitcast(F32), SUB,
                       s["w_lo_ready"])
                chunk[0] = max(chunk[0], upto)

            def normed(n, src, dst, gain=None):
                dve.wait_ge(s["rstd_ready"], n + 1)
                for c in range(KD):
                    if gain is None:
                        tt(dst(c), src(c), rstd_of(n), MUL, s["scaled_ready"])
                    else:
                        stt(dst(c), src(c), gain(c), rstd_of(n), MUL, MUL, s["h_ready"])

            def add_normed(n, gain):
                dve.wait_ge(s["rstd_ready"], n + 1)
                for j in range(4):
                    for c in (2 * j, 2 * j + 1):
                        i = stt(M[:, c, :], M[:, c, :], gain(c), rstd[:, :], MUL, MUL)
                    settle(i)
                    x2 = X[:, 2 * j:2 * j + 2, :]
                    tt(x2, x2, M[:, 2 * j:2 * j + 2, :], ADD, s["x_ready"])

            def gain_of(i):
                return lambda c: col("norm_g", i * KD + c)

            def input_lo(i):
                for c in range(KD):
                    dve.wait_ge(s["in_hi_ready"], KD * i + c + 1)
                    tt(in_lo[:, c, :], H[:, c, :], in_hi[:, c, :].bitcast(F32), SUB, s["in_lo_ready"])

            dve.memset(ones[:, :], 1.0).then_inc(s["ones_set"], 1)
            dve.wait_ge(s["ld_vec"], 16)
            dve.wait_ge(s["ld_x"], 16)
            normed(0, lambda c: X[:, c, :], lambda c: H[:, c, :], gain_of(0))
            weights_lo(1)
            input_lo(0)
            weights_lo(CHUNK_AT["ffn_in0"][0])
            ap = col("a_param", 0, KL)
            stt(lsp[:, 0, :], ap, -1.0, ap, MUL, MAX, s["lsp_dve"])
            dve.wait_ge(s["lsp_act"], 1)
            ts(lsp[:, 1, :], lsp[:, 0, :], 1.0, ADD, inc=s["lsp_dve"])
            dve.wait_ge(s["lsp_act"], 2)
            settle(ts(nsp8, ap, -1.0, MUL))
            log1p_end(lsp[:, 0, :], lsp[:, 1, :], lsp[:, 2, :], nsp8, sp8)
            settle(ts(sp8, sp8, 8.0, MUL))
            ts(nsp8, sp8, -1.0, MUL, inc=s["lsp_dve"])
            dve.wait_ge(s["ld_ret"], 16)
            for kind, dst in (("q", q), ("k", k)):
                for h in range(HEADS):
                    t = TILE[kind, h]
                    await_full(dve, t)
                    if t > TILE["q", 0]:
                        dve.wait_ge(s["rope_done"], t - TILE["q", 0])
                    tt(rope_tmp[:, 0, :], bank(t), rcos, MUL)
                    i = tt(rope_tmp[:, 1, :], bank(t), rsin, MUL, bank_read[t % ROT])
                    await_read(dve, t)
                    tt(dst[:, 2 * h, :], rope_tmp[:, 0, 0:T], rope_tmp[:, 1, T:2 * T], SUB)
                    tt(dst[:, 2 * h + 1, :], rope_tmp[:, 0, T:2 * T], rope_tmp[:, 1, 0:T], ADD, s["rope_done"])

            def decayed(h):
                t = TILE[f"s{h}", 0]
                await_full(dve, t)
                tt(sT[:, h % 2, :], bank(t)[:, 0:384], decay[:, h, :], MUL, bank_read[t % ROT])

            def head_norm(h):
                for tau in range(2):
                    j, t = 2 * h + tau, TILE[f"o{h}", tau]
                    await_full(dve, t)
                    settle(dve.bn_stats(ost[:, j, :], bank(t)))
                    dve.bn_aggr(omv[:, j, :], ost[:, j, :]).then_inc(s["omv_ready"], 1)
                for tau in range(2):
                    j, t = 2 * h + tau, TILE[f"o{h}", tau]
                    dve.wait_ge(s["osd_ready"], j + 1)
                    settle(dve.reciprocal(ors[:, j:j + 1], osd[:, j:j + 1]))
                    ts(on[:, j % 4, :], bank(t), omv[:, j, 0:1], SUB, ors[:, j:j + 1], MUL, bank_read[t % ROT])

            def gated(h):
                for tau in range(2):
                    t = TILE[f"t{h}", tau]
                    await_full(dve, t)
                    if h == 0:
                        for j in range(8):
                            await_read(dve, TILE["g", j])
                    g4 = sg[:, 4 * h:4 * h + 4, tau * P:(tau + 1) * P]
                    tt(g4, g4, cut(bank(t), 4, P), MUL, bank_read[t % ROT])

            for step, h in ((decayed, 0), (decayed, 1), (head_norm, 0), (decayed, 2), (head_norm, 1), (gated, 0),
                            (decayed, 3), (head_norm, 2), (gated, 1), (head_norm, 3), (gated, 2), (gated, 3)):
                step(h)
            add_normed(1, gain_of(1))
            weights_lo(CHUNK_AT["ffn_in0"][0] + 2)
            normed(2, lambda c: X[:, c, :], lambda c: H[:, c, :], gain_of(2))

            def ffn(layer):
                input_lo(2 * layer + 1)
                for j in range(KF // 2):
                    tg, tu = TILE[f"ffn_in{layer}", 2 * j], TILE[f"ffn_in{layer}", 2 * j + 1]
                    weights_lo(chunks_by(f"ffn_in{layer}", 2 * j + 1))
                    await_read(dve, tg)
                    await_full(dve, tu)
                    hid, hi = cut(act2[:, j % 2, :], 2, T), hid_hi[:, 2 * j:2 * j + 2, :]
                    settle(tt(hid, hid, cut(bank(tu), 2, T), MUL))
                    settle(dve.tensor_copy(hi, hid))
                    tt(hid_lo[:, 2 * j:2 * j + 2, :], hid, hi.bitcast(F32), SUB, bank_read[tu % ROT])
                first, count = CHUNK_AT[f"ffn_out{layer}"]
                weights_lo(first + count)

            ffn(0)
            add_normed(3, gain_of(3))
            weights_lo(CHUNK_AT["lru_u"][0] + 2)
            normed(4, lambda c: X[:, c, :], lambda c: H[:, c, :], gain_of(4))
            input_lo(2)
            await_full(dve, TILE["ffn_out0", 3])
            dve.memset(upad[:, :, 0:LPAD], 0.0).then_inc(s["pads_zero"], 1)
            for i in range(KL):
                weights_lo(chunks_by("lru_u" if i < KL // 2 else "lru_y", i % (KL // 2)))
                await_read(dve, TILE["lru_u", i // 2])
                wk = [col("lconv_w", kk * KL + i) for kk in range(LCONV)]
                settle(ts(uc[:, i, :], upad[:, i, 0:T], wk[0], MUL, col("lconv_b", i), ADD))
                for kk in range(1, LCONV):
                    x = stt(uc[:, i, :], upad[:, i, kk:kk + T], wk[kk], uc[:, i, :], MUL, ADD,
                            s["uc_ready"] if kk == LCONV - 1 else None)
                    if kk < LCONV - 1:
                        settle(x)

            def four(v, n):
                return v[:, 4 * n:4 * n + 4, :]

            await_read(dve, TILE["lru_gate", KL - 1])
            dve.wait_ge(s["uc_ready"], KL)
            for n in range(3):
                x = tt(four(li, n), four(li, n), four(uc, n), MUL)
            settle(x)
            for n in range(3):
                dve.wait_ge(s["a_ready"], n + 1)
                settle(tt(four(uc, n), four(la, n), four(la, n), MUL))
                dve.wait_ge(s["th_ready"], n + 1)
                stt(four(uc, n), four(uc, n), 1.0, r_tiles(4 * n, 4), ADD, MUL, s["lsq_arg"])
            for n in range(3):
                dve.wait_ge(s["lsq_ready"], n + 1)
                settle(tt(four(li, n), four(li, n), four(uc, n), MUL))
                for i in range(4 * n, 4 * n + 4):
                    x = dve.tensor_tensor_scan(uc[:, i, :], la[:, i, :], li[:, i, :], 0.0, MUL, ADD)
                settle(x)
                if n == 0:
                    for j in range(KL // 2):
                        await_read(dve, TILE["lru_y", j])
                tt(four(li, n), four(uc, n), four(gy, n), MUL, s["go_ready"])
            add_normed(5, gain_of(5))
            weights_lo(CHUNK_AT["ffn_in1"][0] + 2)
            normed(6, lambda c: X[:, c, :], lambda c: H[:, c, :], gain_of(6))
            ffn(1)
            add_normed(7, gain_of(7))
            dve.wait_ge(s["mod_full"], 12)
            bm = col("b_mod", 0, 6 * KD).unsqueeze(2).to_broadcast([P, 6 * KD, 2])
            settle(tt(mod[:, :, :], ps[:, MODB, 0:12 * KD].rearrange("p (a b) -> p a b", b=2), bm, ADD))
            for n, (chunk, which, gain) in enumerate(((1, 1, "norm1"), (1, 0, "norm1"), (4, 0, "norm2"))):
                i = stt(coef[:, n, :], mod[:, chunk * KD:(chunk + 1) * KD, which], 1.0, col(gain, 0, KD), ADD, MUL)
            settle(i)
            dve.wait_ge(s["ld_ctx"], 16)
            normed(8, lambda c: ctxT[:, c, :], lambda c: hcat[:, c, 0:T])
            normed(9, lambda c: X[:, c, :], lambda c: hcat[:, c, T:2 * T])
            dve.memset(pad3[:, :, :, 0:CPAD], 0.0)
            dve.memset(pad3[:, :, :, CPAD + T:], 0.0).then_inc(s["pads_zero"], 1)

            def conv(m):
                lo = 0 if m < KX + KB else 1
                await_read(dve, TILE["ssd_in", m])
                if m >= 2:
                    dve.wait_ge(s["wt_ready"], m - 1)
                o = conv2[:, m % 2, lo:2, :]
                src = [pad3[:, m % 3, lo:2, kk:kk + T] for kk in range(CONV)]
                settle(ts(o, src[0], col("conv_w", m), MUL, col("conv_b", m), ADD))
                for kk in range(1, CONV):
                    x = stt(o, src[kk], col("conv_w", kk * 16 + m), o, MUL, ADD,
                            s["conv_ready"] if kk == CONV - 1 else None)
                    if kk < CONV - 1:
                        settle(x)

            for m in range(KX + KB):
                conv(m)
            t = TILE["ssd_dt", 0]
            await_full(dve, t)
            ts(dtx, bank(t)[0:ND, :], col("dt_bias", rows=ND), ADD, inc=bank_read[t % ROT])
            for m in range(KX + KB, KX + 2 * KB):
                conv(m)
            await_read(dve, t)
            dve.wait_ge(s["wt_ready"], KX + 2 * KB)
            stt(dtb, dtx, -1.0, dtx, MUL, MAX, s["dt_dve"])
            dve.wait_ge(s["dt_act"], 2)
            ts(dtc, dtb, 1.0, ADD, inc=s["dt_dve"])
            dve.wait_ge(s["dt_act"], 3)
            log1p_end(dtb, dtc, dta, dtx, scr)
            settle(ts(sneg, elog, -1.0, MUL))
            dve.memset(dtb, 1.0)
            settle(ts(dta, scr, sneg, MUL))
            for half in range(2):
                lo, hi = half * T, half * T + T
                dst = dtc[:, 0:T] if half == 0 else a_lat[:, :]
                fw = dtc[:, T:2 * T]
                settle(dve.tensor_tensor_scan(fw, dtb[:, 0:T], dta[:, lo:hi], 0.0, MUL, ADD))
                if half == 0:
                    ts(stot, fw[:, T - 1:T], 1.0, MUL)
                settle(dve.tensor_tensor_scan(dtx[:, 0:T][:, ::-1], dtb[:, 0:T], dta[:, lo:hi][:, ::-1], 0.0, MUL, ADD))
                settle(ts(dst, fw, col("forward", rows=ND), MUL))
                settle(stt(dst, dtx[:, 0:T], col("backward", rows=ND), dst, MUL, ADD))
            ts(dtc[:, 0:T], dtc[:, 0:T], stot, SUB, -1.0, MUL, inc=s["dt_dve"])
            dve.wait_ge(s["dt_act"], 4)
            tt(dtx[:, 0:T], dtc[:, 0:T], scr[:, 0:T], MUL)
            ts(dtx[:, T:2 * T], scr[:, T:2 * T], 1.0, MUL, inc=s["dt_ready"])
            t = TILE["dt_tok", 0]
            await_full(dve, t)
            dve.tensor_copy(tok6[:, :, :].rearrange("p a b -> p (a b)"), bank(t)[:, 0:6 * ND]).then_inc(bank_read[t % ROT], 1)
            await_read(dve, t)
            ts(nega[:, :, :], tok6[:, 0:2, :], -1.0, MUL, inc=s["tok6_ready"])
            for m in range(KX):
                await_read(dve, TILE["turn", m])
            await_full(dve, TILE["ssd_f", 1])
            for d in range(2):
                for tau in range(2):
                    w16 = tok6[:, 4 + tau, d * SH:(d + 1) * SH].unsqueeze(2).to_broadcast([P, SH, SP_])
                    tt(cut(xw[:, 2 * d + tau, :], SH, SP_), cut(xs_tok[:, tau, :], SH, SP_), w16, MUL, s["xw_ready"])
            def y_out(pair):
                t = TILE["y", pair]
                await_full(dve, t)
                yx = xs_lat[:, pair, :]
                stt(yx, yx, col("d_skip", pair), bank(t)[:, 0:T], MUL, ADD, bank_read[t % ROT])
                await_read(dve, t)
                if pair == 0:
                    for j in range(4):
                        await_read(dve, TILE["ssd_z", j])
                tt(yx, yx, mix[:, pair, :], MUL, s["y_ready"])

            dve.wait_ge(s["ld_ssd"], 16)
            await_full(dve, TILE["state", SG_ - 1])
            for h in range(SH):
                if h % 4 == 0:
                    t = TILE["cb", h // 4]
                    await_full(dve, t)
                    if h:
                        dve.wait_ge(s["m_ready"], h)
                    bk = bank(t)
                    dve.tensor_copy(cbx[:, 0, 0:T], bk[:, 0:T])
                    dve.tensor_copy(cbx[:, 0, T:384], bk[:, 0:P])
                    dve.tensor_copy(cbx[:, 1, 0:P], bk[:, T + P:2 * T])
                    dve.tensor_copy(cbx[:, 1, P:384], bk[:, T:2 * T]).then_inc(bank_read[t % ROT], 1)
                    await_read(dve, t)
                t = TILE["row", h]
                dve.wait_ge(s["ea_ready"], h + 1)
                for j in range(2):
                    tt(rmask[:, h % 2, j, :], bank(t)[:, j * P:j * P + 384], smask[:, j, :], ADD,
                       bank_read[t % ROT] if j == 1 else None)
                cg = c_lat[:, h // 4:h // 4 + 1, :].to_broadcast([P, 2, T])
                if h >= 2:
                    if h % 2 == 0:
                        dve.wait_ge(s["even_head"], h // 2)
                    else:
                        await_full(dve, TILE["y", (h - 2) // 2])
                tt(cut(ce[:, h % 2, :], 2, T), cut(act2[:, h % 2, :], 2, T), cg, MUL)
                dve.wait_ge(s["dec_ready"], h + 1)
                dm = decm[:, h % 2]
                for j in range(2):
                    mid = T - j * P
                    stt(dm[:, j, 0:mid], dm[:, j, 0:mid], tok6[:, 2 + j, h:h + 1], cbx[:, j, 0:mid], MUL, MUL)
                    stt(dm[:, j, mid:384], dm[:, j, mid:384], tok6[:, 2 + j, SH + h:SH + h + 1], cbx[:, j, mid:384], MUL,
                        MUL, s["m_ready"] if j == 1 else None)
                if h % 2 == 0 and h >= 2:
                    y_out(h // 2 - 1)
            y_out(KX - 1)
            normed(10, lambda c: xs_lat[:, c, :], lambda c: mix[:, c, :], lambda c: col("ssd_norm", c))
            for j in range(4):
                t = TILE["mix_out", j]
                await_full(dve, t)
                for m in range(2):
                    c = 2 * j + m
                    stt(X[:, c, :], bank(t)[:, m * T:(m + 1) * T], mod[:, 2 * KD + c, 0:1], X[:, c, :], MUL, ADD,
                        bank_read[t % ROT] if m == 1 else None)
            normed(11, lambda c: X[:, c, :], lambda c: H[:, c, :])
            dve.memset(macc[:, :, :], 0.0)
            dve.memset(yp, 0.0).then_inc(s["yp_ready"], 1)
            dve.memset(SGt[:, 0, :], 0.0).then_inc(s["sc_free"], 1)
            dve.memset(SGt[:, 1, :], 0.0).then_inc(s["sc_free"], 1)
            t = TILE["route", 0]
            await_full(dve, t)
            bias = col("b_route", 0, NG + NE).unsqueeze(1).to_broadcast([P, 2, NG + NE])
            tt(logits[:, :, :], cut(bank(t)[:, 0:128], 2, 64)[:, :, 0:NG + NE], bias, ADD, bank_read[t % ROT])
            await_read(dve, t)

            def wide(x, n):
                return x.unsqueeze(2).to_broadcast([P, 2, n])

            def reduce(o, x, op):
                return dve.tensor_reduce(o, x, AX_X, op)

            def first_max(o, x, top, tmp, n):
                settle(reduce(top, x, MAX))
                settle(tt(o, x, wide(top, n), EQ))
                settle(tt(o, o, col("desc", NJ - n, n).unsqueeze(1).to_broadcast([P, 2, n]), MUL))
                settle(reduce(tmp, o, MAX))
                settle(tt(o, o, wide(tmp, n), EQ))

            def r2(i):
                return rt[:, i, 0:2]

            def r2n(i, n):
                return cut(rt[:, i, 0:2 * n], 2, n)

            lg = logits[:, :, 0:NG]
            top, tmp, og = r2(2), r2(3), r2n(4, NG)
            first_max(og, lg, top, tmp, NG)
            tt(r2n(0, NG), lg, wide(top, NG), SUB, s["exp_arg"])
            pick = rt[:, 16, 0:64].rearrange("p (t j g) -> p t j g", t=2, g=NG)
            le = logits[:, :, NG:NG + NE].rearrange("p t (g j) -> p t j g", g=NG)
            for tau in range(2):
                i = tt(pick[:, tau], le[:, tau], og[:, tau:tau + 1, :].to_broadcast([P, NJ, NG]), MUL)
            settle(i)
            ls, o1, o2, ls2 = r2n(5, NJ), r2n(6, NJ), r2n(7, NJ), r2n(8, NJ)
            for tau in range(2):
                i = reduce(ls[:, tau, :], pick[:, tau], ADD)
            settle(i)
            first_max(o1, ls, r2(9), tmp, NJ)
            settle(stt(ls2, o1, -3.0e38, ls, MUL, ADD))
            first_max(o2, ls2, r2(10), tmp, NJ)
            tt(r2(13), r2(10), r2(9), SUB, s["exp_arg"])
            settle(tt(r2n(11, NJ), o1, o2, ADD))
            for tau in range(2):
                i = tt(cut(msk[:, tau, :], NG, NJ), og[:, tau, :].unsqueeze(2).to_broadcast([P, NG, NJ]),
                       r2n(11, NJ)[:, tau:tau + 1, :].to_broadcast([P, NG, NJ]), MUL,
                       s["msk_ready"] if tau == 1 else None)
            dve.wait_ge(s["exp_ready"], 2)
            settle(reduce(r2(12), r2n(1, NG), ADD))
            settle(ts(r2(15), r2(14), 1.0, ADD))
            settle(tt(r2(12), r2(12), r2(15), MUL))
            settle(dve.reciprocal(r2(17), r2(12)))
            settle(tt(r2(18), r2(17), r2(14), MUL))
            settle(tt(r2n(19, NJ), o1, wide(r2(17), NJ), MUL))
            settle(tt(r2n(20, NJ), o2, wide(r2(18), NJ), MUL))
            settle(tt(r2n(21, NJ), r2n(19, NJ), r2n(20, NJ), ADD))
            for tau in range(2):
                i = tt(cut(gw[:, tau, :], NG, NJ), og[:, tau, :].unsqueeze(2).to_broadcast([P, NG, NJ]),
                       r2n(21, NJ)[:, tau:tau + 1, :].to_broadcast([P, NG, NJ]), MUL)
            settle(i)
            t = TILE["route", 1]
            await_full(dve, t)
            dve.wait_ge(s["msk_ready"], 1)
            settle(stt(pos1[:, :, :], cut(bank(t)[:, 0:2 * NE], 2, NE), 1.0, msk[:, :, :], ADD, MUL))
            pP = posP[:, 0:NE // 2, :].rearrange("p a (t e) -> p t a e", t=2)
            gP = gateP[:, 0:NE // 2, :].rearrange("p a (t e) -> p t a e", t=2)
            for tau in range(2):
                ts(pP[:, tau], cut(pos1[:, tau, :], NE // 2, 2), 1.0, SUB)
                i = ts(gP[:, tau], cut(gw[:, tau, :], NE // 2, 2), 1.0, MUL)
            settle(i)
            ts(posP[:, NE // 2, :], posP[:, 0, :], float(CAP), SUB)
            settle(dve.tensor_copy(gateP[:, NE // 2, :], gateP[:, 0, :]))
            settle(reduce(rt[:, 22, 0:1], bank(t)[:, 2 * NE:3 * NE], MAX))
            settle(ts(rt[:, 22, 1:2], rt[:, 22, 0:1], float(CAP), ALU.is_gt, 1.0, ADD))
            for n in range(2, T // CAP):
                settle(stt(rt[:, 22, 1:2], rt[:, 22, 0:1], float(CAP * n), rt[:, 22, 1:2], ALU.is_gt, ADD))
            dve.tensor_copy(rounds[:, 0:1], rt[:, 22, 1:2]).then_inc(s["route_ready"], 1)
            dve.wait_ge(s["route_ready"], 1)
            ts(rt[:, 23, 0:1], rt[:, 22, 0:1], 1.0, MUL, inc=s["moe_init"])
            n_rounds = dve.value_load(rounds[0:1, 0:1], min_val=1, max_val=T // CAP)
            iota4 = iota[:, :].unsqueeze(1).to_broadcast([P, 4, CAP])

            def scatter_add(use0, n0):
                for part in range(4):
                    dve.wait_ge(s["sc_full"], use0 + (n0 + part + 1))
                    m2 = macc[:, 2 * part:2 * part + 2, :]
                    tt(m2, m2, cut(ps[:, 6 + (n0 + part) % 2, :], 2, T), ADD, s["sc_free"])

            def select(lo, par, count):
                pc = posP.rearrange("p a b -> p (a b)")[:, bass.ds(lo, 4)].unsqueeze(2).to_broadcast([P, 4, CAP])
                gc = gateP.rearrange("p a b -> p (a b)")[:, bass.ds(lo, 4)].unsqueeze(2).to_broadcast([P, 4, CAP])
                tt(cut(S2[:, par, :], 4, CAP), iota4, pc, EQ, s["eq_ready"])
                dve.wait_ge(s["eq_ready"], count)
                tt(cut(SGb[:, par, :], 4, CAP), cut(S2[:, par, :], 4, CAP), gc, MUL, s["sel_ready"])

            select(0, 0, 1)
            with dve.Fori(0, n_rounds) as r:
                with dve.Fori(0, EXPERT_UNITS // BODY) as b:
                    turns = r * (EXPERT_UNITS // BODY) + b
                    for par in range(2):
                        pair = turns * 2 + par
                        select(b * 8 + 4 * par + 4, 1 - par, pair + 2)
                        scatter_add(turns * 10, 5 * par)
                        dve.wait_ge(s["gs_ready"], pair + 1)
                        dve.wait_ge(s["gu_full"], pair * 2 + 2)
                        tt(hs, gs, ps[:, 1, :], MUL, s["hs_ready"])
                        dve.wait_ge(s["sc_full"], turns * 10 + (5 * par + 5))
                        dve.tensor_copy(SGt[:, par, :], ps[:, 6 + (5 * par + 4) % 2, 0:T]).then_inc(s["sc_free"], 1)
                dve.wait_ge(s["sel_ready"], (r + 1) * (NE // 2) + 1)
                ts(posP.rearrange("p a b -> p (a b)"), posP.rearrange("p a b -> p (a b)"), float(CAP), SUB,
                   inc=s["moe_init"])
                dve.wait_ge(s["moe_init"], r + 2)
            scatter_add(n_rounds * (5 * NE // 2), 0)
            dve.wait_ge(s["sc_free"], n_rounds * (5 * NE // 2) + 6)
            for c in range(KD):
                stt(X[:, c, :], macc[:, c, :], mod[:, 5 * KD + c, 0:1], X[:, c, :], MUL, ADD,
                    s["x_ready"] if c % 2 == 1 else None)
            normed(12, lambda c: X[:, c, :], lambda c: H[:, c, :], lambda c: col("final", c))


def _units(x):
    n = -(-x.shape[1] // UNIT)
    if n * UNIT != x.shape[1]:
        x = np.concatenate([x, np.zeros((P, n * UNIT - x.shape[1]), x.dtype)], 1)
    return x.reshape(P, n, UNIT).transpose(1, 0, 2)


def _blocks(w, tiles=None):
    kt, mt = w.shape[0] // P, w.shape[1] // P
    x = w.reshape(kt, P, mt, P).transpose(1, 2, 0, 3)
    if tiles is not None:
        x = x[:, tiles]
    return _units(x.reshape(P, -1))


def _rows(w):
    return w.reshape(-1, P, w.shape[1]).transpose(1, 0, 2)


def _cols(x):
    return np.moveaxis(x.reshape(*x.shape[:-1], -1, P), -1, 0).reshape(P, -1)


def _constants():
    f = np.float32
    tok = np.arange(T)
    inv = (f(1.0) / (f(10000.0) ** (np.arange(DK // 2, dtype=f) / f(DK // 2)))).astype(f)
    ang = (tok.astype(f)[None, :] * inv[:, None]).astype(f).astype(np.float64)
    ret = np.zeros((P, 2560), f)
    ret[:, 0:512] = np.tile(np.cos(ang), 2)
    ret[:, 512:1024] = np.tile(np.sin(ang), 2)
    key, query = np.arange(P)[:, None], np.concatenate([tok, np.arange(P)])[None, :]
    for h in range(HEADS):
        lg = np.log1p(-np.exp2(-5.0 - h))
        rel = (query - key).astype(np.float64)
        ret[:, 1024 + 384 * h:1408 + 384 * h] = np.where(rel >= 0, np.exp(np.maximum(rel, 0) * lg), 0) * DK ** -0.5
    ssd = np.zeros((P, 2048), f)
    ch = 2 * np.pi * (np.outer(np.arange(P), np.arange(P)) % P) / P
    ssd[:, 0:P], ssd[:, P:256] = np.cos(ch), np.sin(ch)
    ln = 2 * np.pi * (np.outer(tok, tok) % T) / T
    norm = (T * P) ** -0.5
    for tau in range(2):
        ssd[:, 256 + T * tau:256 + T * (tau + 1)] = np.cos(ln[tau * P:(tau + 1) * P]) * norm
        ssd[:, 768 + T * tau:768 + T * (tau + 1)] = -np.sin(ln[tau * P:(tau + 1) * P]) * norm
    off = f(-1.0e30)
    for j in range(2):
        kk = np.arange(P)[:, None] + j * P
        fw, bw = (tok[None, :] if j == 0 else tok[None, P:]), (tok[None, :P] if j == 0 else tok[None, :])
        ssd[:, 1280 + 384 * j:1664 + 384 * j] = np.concatenate(
            [np.where(fw >= kk, f(0), off), np.where(bw <= kk, f(0), off)], 1)
    glob = np.concatenate([np.tile(np.arange(CAP, dtype=f), (P, 1)), np.eye(P, dtype=f),
                           np.triu(np.ones((P, P), f), 1)], 1)
    return ret, ssd, glob


def _layout(i):
    one = {n: np.asarray(x) for n, x in i.items()}
    wr = one["ret_w_in"][0]
    lo = 2 * HEADS * DK
    hv = HEADS * DV
    ffn_order = [t for j in range(KF // 2) for t in (2 * j, 2 * j + 1, KF + 2 * j, KF + 2 * j + 1)]
    gate = one["lru_gate_w"][0]
    gate_units = []
    for u in range(2):
        x = gate[:, 3 * u:3 * u + 3].reshape(2, 3, 2, P, 2, P)
        gate_units.append(_units(x.transpose(3, 1, 0, 4, 2, 5).reshape(P, -1)))
    wi = one["w_in_2"][0]
    z0, x0 = 0, D
    b0 = x0 + D
    c0 = b0 + SG_ * SN
    t0 = c0 + SG_ * SN
    f0 = t0 + ND
    parts = {
        "mod": _blocks(one["w_mod_2"][0]),
        "ret_q": _blocks(wr[:, 0:D]), "ret_k": _blocks(wr[:, D:lo]), "ret_g": _blocks(wr[:, lo + hv:]),
        "ret_v": np.concatenate([_units(_rows(wr[:, lo + h * DV:lo + (h + 1) * DV]).reshape(P, -1)) for h in range(HEADS)]),
        "ret_out": _blocks(one["ret_w_out"][0]),
        "lru_y": _blocks(one["lru_w_in"][0][:, 0:LW]), "lru_u": _blocks(one["lru_w_in"][0][:, LW:]),
        "lru_gate": np.concatenate(gate_units), "lru_out": _blocks(one["lru_w_out"][0]),
        "ssd_xs": _blocks(wi[:, x0:b0]), "ssd_b": _blocks(wi[:, b0:c0]), "ssd_c": _blocks(wi[:, c0:t0]),
        "ssd_z": _blocks(wi[:, z0:x0]), "ssd_f": _blocks(wi[:, f0:]), "mix_out": _blocks(one["w_out_2"][0]),
    }
    for layer in range(2):
        parts[f"ffn_in{layer}"] = _blocks(one["ffn_w_in"][layer], ffn_order)
        parts[f"ffn_out{layer}"] = _blocks(one["ffn_w_out"][layer])
    dense = np.concatenate([parts[name][first:first + n] for name, first, n in STREAM])
    experts = []
    for e in range(0, NE, 2):
        for name in ("w_eg_2", "w_eu_2", "w_ed_2"):
            experts += [_units(_rows(one[name][0, x]).reshape(P, -1)) for x in (e, e + 1)]

    vec = np.zeros((P, NVEC), np.float32)

    def put(name, x, rows=P):
        off, n = VOFF[name]
        vec[0:rows, off:off + n] = x

    put("norm_g", _cols(one["norm_g"]))
    put("lconv_w", _cols(one["lru_conv_w"][0]))
    put("lconv_b", _cols(one["lru_conv_b"][0]))
    put("lgate_b", _cols(one["lru_gate_b"][0].reshape(2, LW)))
    put("a_param", _cols(one["lru_a_param"][0]))
    put("b_mod", _cols(one["b_mod_2"][0]))
    put("norm1", _cols(one["norm1_2"][0]))
    put("conv_w", _cols(one["conv_w_2"][0]))
    put("conv_b", _cols(one["conv_b_2"][0]))
    put("d_skip", _cols(np.repeat(one["d_skip_2"][0], SP_)))
    put("ssd_norm", _cols(one["ssd_norm_2"][0]))
    put("norm2", _cols(one["norm2_2"][0]))
    put("final", _cols(one["final_norm_2"]))
    put("c", np.stack([_cols(one["c_2"][0]), _cols(one["c_ctx_2"])], 2).reshape(P, -1))
    put("b_route", np.broadcast_to(np.concatenate([one["b_rg_2"][0], one["b_re_2"][0].reshape(-1)]), (P, NG + NE)))
    put("dt_bias", one["dt_bias_2"][0].reshape(ND, 1), ND)
    put("a_log", one["a_log_2"][0].reshape(ND, 1), ND)
    put("eps", np.float32(EPS))
    put("desc", np.arange(NJ, 0, -1, dtype=np.float32))
    put("forward", np.ones((SH, 1), np.float32), SH)
    put("backward", (np.arange(ND) >= SH).astype(np.float32)[:, None], ND)
    ret, ssd, glob = _constants()
    wroute = np.concatenate([one["w_rg_2"][0], one["w_re_2"][0].transpose(1, 0, 2).reshape(D, NE)], 1)
    return {
        "vec": vec, "x": _rows(one["x"][0].T), "ctx": _rows(one["ctx_2"][0].T), "dense": dense,
        "experts": np.concatenate(experts), "ret_cst": ret, "ssd_cst": ssd, "glob": glob,
        "wdt": _rows(wi[:, t0:f0]), "wfour": one["w_four_2"][0].transpose(1, 0, 2), "wroute": _rows(wroute),
    }


def kernel(**inputs):
    from concourse import bacc
    from concourse.bass_utils import run_bass_kernel_spmd

    nc = bacc.Bacc("TRN2", target_bir_lowering=False, num_devices=1)
    arrays = {f"in_{n}": np.ascontiguousarray(x) for n, x in _layout(inputs).items()}
    dram = {n[3:]: nc.dram_tensor(n, x.shape, F32, kind="ExternalInput").ap() for n, x in arrays.items()}
    out = nc.dram_tensor("out", (P, KD, T), F32, kind="ExternalOutput").ap()
    two_blocks(nc, dram, out)
    y = run_bass_kernel_spmd(nc, [arrays], core_ids=[0]).results[0]["out"]
    return np.ascontiguousarray(y.transpose(2, 1, 0)).reshape(1, T, D)
```
